# Optimizing a Trainium2 kernel written in Bass

```python
import math
import jax, jax.numpy as jnp
from jax import lax
import numpy as np

D_MODEL = 1024
BATCH = 1
SEQ = 256
DEPTH = 2

CHUNK = 64
Q_BLOCK = 128
N_A_LAYERS = DEPTH // 2
N_B_LAYERS = DEPTH - N_A_LAYERS
SSM_GROUP = 16
SSM_GROUPS = D_MODEL // SSM_GROUP
SSM_STATE = 64
DT_MIN = 0.001
DT_MAX = 0.1
N_HEADS = 16
QK_NOPE_DIM = 64
QK_ROPE_DIM = 32
V_HEAD_DIM = 64
Q_LORA_RANK = 256
KV_LORA_RANK = 256
ROPE_THETA = 10000.0
ATTN_SCALE = 1.0 / math.sqrt(QK_NOPE_DIM + QK_ROPE_DIM)
D_FF = ((8 * D_MODEL + 3 * 256 - 1) // (3 * 256)) * 256
EPS = 1e-6


def rms_norm(x, g):
    xf = x.astype(jnp.float32)
    y = xf * lax.rsqrt(jnp.mean(xf * xf, axis=-1, keepdims=True) + EPS)
    return (y * g.astype(jnp.float32)).astype(x.dtype)

def modulate(h, shift, scale):
    return h * (1.0 + scale[:, None, :]) + shift[:, None, :]

def rope_cos_sin(positions):
    inv = 1.0 / (ROPE_THETA ** (jnp.arange(0, QK_ROPE_DIM, 2, dtype=jnp.float32) / QK_ROPE_DIM))
    ang = positions.astype(jnp.float32)[..., None] * inv
    return jnp.cos(ang), jnp.sin(ang)

def apply_rope(x, cos, sin):
    shape = cos.shape[:2] + (1,) * (x.ndim - 3) + cos.shape[-1:]
    cos = cos.reshape(shape)
    sin = sin.reshape(shape)
    x1, x2 = jnp.split(x.astype(jnp.float32), 2, axis=-1)
    return jnp.concatenate([x1 * cos - x2 * sin, x1 * sin + x2 * cos], axis=-1).astype(x.dtype)

def _complex_linear_combine(e1, e2):
    a1r, a1i, b1r, b1i = e1
    a2r, a2i, b2r, b2i = e2
    ar = a1r * a2r - a1i * a2i
    ai = a1r * a2i + a1i * a2r
    br = a2r * b1r - a2i * b1i + b2r
    bi = a2r * b1i + a2i * b1r + b2i
    return (ar, ai, br, bi)

def s5_mixer(h, lam_re, lam_im, log_dt, b_re, b_im, c_re, c_im, d_skip, w_glu, b_glu):
    bsz, s_len, d = h.shape
    f32 = jnp.float32
    lr = lam_re.astype(f32)
    li = lam_im.astype(f32)
    dt = jnp.exp(log_dt.astype(f32))[:, None]
    mag = jnp.exp(lr * dt)
    ab_re = mag * jnp.cos(li * dt)
    ab_im = mag * jnp.sin(li * dt)
    den = lr * lr + li * li
    nr = ab_re - 1.0
    ni = ab_im
    f_re = (nr * lr + ni * li) / den
    f_im = (ni * lr - nr * li) / den
    br = b_re.astype(f32)
    bi = b_im.astype(f32)
    bb_re = f_re[..., None] * br - f_im[..., None] * bi
    bb_im = f_re[..., None] * bi + f_im[..., None] * br
    cr = c_re.astype(f32)
    ci = c_im.astype(f32)

    n_chunks = s_len // CHUNK
    u = h.astype(f32).reshape(bsz, n_chunks, CHUNK, SSM_GROUPS, SSM_GROUP).transpose(1, 0, 2, 3, 4)

    def chunk_step(carry, u_c):
        s_re, s_im = carry
        bu_re = jnp.einsum('blgp,gnp->blgn', u_c, bb_re)
        bu_im = jnp.einsum('blgp,gnp->blgn', u_c, bb_im)
        a_re = jnp.broadcast_to(ab_re, bu_re.shape)
        a_im = jnp.broadcast_to(ab_im, bu_im.shape)
        pa_re, pa_im, loc_re, loc_im = lax.associative_scan(
            _complex_linear_combine, (a_re, a_im, bu_re, bu_im), axis=1)
        st_re = loc_re + pa_re * s_re[:, None] - pa_im * s_im[:, None]
        st_im = loc_im + pa_re * s_im[:, None] + pa_im * s_re[:, None]
        y = jnp.einsum('blgn,gpn->blgp', st_re, cr) - jnp.einsum('blgn,gpn->blgp', st_im, ci)
        return (st_re[:, -1], st_im[:, -1]), y

    init = (jnp.zeros((bsz, SSM_GROUPS, SSM_STATE), f32), jnp.zeros((bsz, SSM_GROUPS, SSM_STATE), f32))
    _, y = lax.scan(chunk_step, init, u)
    y = y.transpose(1, 0, 2, 3, 4).reshape(bsz, s_len, d)
    y = (y + d_skip.astype(f32) * h.astype(f32)).astype(h.dtype)
    g = jax.nn.gelu(y)
    return g * jax.nn.sigmoid(g @ w_glu + b_glu)

def shared_mla_kv(hk, cos, sin, w_kv_a, kv_a_norm_g, w_kv_b, k_nope_norm_g, k_rope_norm_g):
    bsz, s_len, _ = hk.shape
    kv_a = hk @ w_kv_a
    c_kv, k_rope = jnp.split(kv_a, [KV_LORA_RANK], axis=-1)
    c_kv = rms_norm(c_kv, kv_a_norm_g)
    kv = (c_kv @ w_kv_b).reshape(bsz, s_len, N_HEADS, QK_NOPE_DIM + V_HEAD_DIM)
    k_nope, v = jnp.split(kv, [QK_NOPE_DIM], axis=-1)
    k_nope = rms_norm(k_nope, k_nope_norm_g)
    k_rope = apply_rope(rms_norm(k_rope, k_rope_norm_g), cos, sin)
    return k_nope, k_rope, v

def mla_attention(h, cos, sin, k_nope, k_rope, v, w_dq, q_norm_g, w_uq, q_nope_norm_g, q_rope_norm_g, w_o):
    bsz, s_len, _ = h.shape
    q = rms_norm(h @ w_dq, q_norm_g) @ w_uq
    q = q.reshape(bsz, s_len, N_HEADS, QK_NOPE_DIM + QK_ROPE_DIM)
    q_nope, q_rope = jnp.split(q, [QK_NOPE_DIM], axis=-1)
    q_nope = rms_norm(q_nope, q_nope_norm_g)
    q_rope = apply_rope(rms_norm(q_rope, q_rope_norm_g), cos, sin)
    n_blocks = s_len // Q_BLOCK
    qn_b = q_nope.reshape(bsz, n_blocks, Q_BLOCK, N_HEADS, QK_NOPE_DIM).transpose(1, 0, 2, 3, 4)
    qr_b = q_rope.reshape(bsz, n_blocks, Q_BLOCK, N_HEADS, QK_ROPE_DIM).transpose(1, 0, 2, 3, 4)
    key_chunk = jnp.arange(s_len) // CHUNK

    def block_attn(args):
        qn, qr, blk = args
        s = (jnp.einsum('bqhd,bkhd->bhqk', qn, k_nope, preferred_element_type=jnp.float32)
             + jnp.einsum('bqhr,bkr->bhqk', qr, k_rope, preferred_element_type=jnp.float32)) * ATTN_SCALE
        q_chunk = (blk * Q_BLOCK + jnp.arange(Q_BLOCK)) // CHUNK
        mask = q_chunk[:, None] >= key_chunk[None, :]
        s = jnp.where(mask[None, None], s, -1e30)
        p = jax.nn.softmax(s, axis=-1)
        return jnp.einsum('bhqk,bkhd->bqhd', p.astype(v.dtype), v)

    o = lax.map(block_attn, (qn_b, qr_b, jnp.arange(n_blocks)))
    o = o.transpose(1, 0, 2, 3, 4).reshape(bsz, s_len, N_HEADS * V_HEAD_DIM)
    return o @ w_o

def swiglu(h, w_gate, w_up, w_down):
    return (jax.nn.silu(h @ w_gate) * (h @ w_up)) @ w_down

def first_inputs(seed: int = 0) -> dict:
    key = jax.random.key(seed)
    ks = iter(jax.random.split(key, 48))
    f32 = jnp.float32
    D, F, G, N, P = D_MODEL, D_FF, SSM_GROUPS, SSM_STATE, SSM_GROUP
    NA, NB = N_A_LAYERS, N_B_LAYERS

    def nrm(shape, scale):
        return jax.random.normal(next(ks), shape, f32) * scale

    def gain(shape):
        return 1.0 + 0.02 * jax.random.normal(next(ks), shape, f32)

    x = jax.random.normal(next(ks), (BATCH, SEQ, D), f32)
    c = jax.random.normal(next(ks), (BATCH, D), f32)
    offsets = jax.random.randint(next(ks), (BATCH, 1), 0, 4096, dtype=jnp.int32)
    positions = offsets + jnp.arange(SEQ, dtype=jnp.int32)[None, :]

    n_idx = jnp.arange(N, dtype=f32)
    inputs = {
        "x": x, "c": c, "positions": positions,
        "ada_w": nrm((DEPTH, D, 6 * D), 0.5 * D ** -0.5),
        "ada_b": nrm((DEPTH, 6 * D), 0.02),
        "norm1_g": gain((DEPTH, D)),
        "norm2_g": gain((DEPTH, D)),
        "ffn_w_gate": nrm((DEPTH, D, F), D ** -0.5),
        "ffn_w_up": nrm((DEPTH, D, F), D ** -0.5),
        "ffn_w_down": nrm((DEPTH, F, D), F ** -0.5),
        "s5_lam_re": -0.5 + 0.01 * jax.random.normal(next(ks), (NA, G, N), f32),
        "s5_lam_im": math.pi * n_idx[None, None, :] + 0.01 * jax.random.normal(next(ks), (NA, G, N), f32),
        "s5_log_dt": jax.random.uniform(next(ks), (NA, G), f32, math.log(DT_MIN), math.log(DT_MAX)),
        "s5_b_re": nrm((NA, G, N, P), P ** -0.5),
        "s5_b_im": nrm((NA, G, N, P), P ** -0.5),
        "s5_c_re": nrm((NA, G, P, N), N ** -0.5),
        "s5_c_im": nrm((NA, G, P, N), N ** -0.5),
        "s5_d": nrm((NA, D), 1.0),
        "s5_w_glu": nrm((NA, D, D), D ** -0.5),
        "s5_b_glu": nrm((NA, D), 0.02),
        "kv_ada_w": nrm((D, 2 * D), 0.5 * D ** -0.5),
        "kv_ada_b": nrm((2 * D,), 0.02),
        "kv_norm_g": gain((D,)),
        "w_kv_a": nrm((D, KV_LORA_RANK + QK_ROPE_DIM), D ** -0.5),
        "kv_a_norm_g": gain((KV_LORA_RANK,)),
        "w_kv_b": nrm((KV_LORA_RANK, N_HEADS * (QK_NOPE_DIM + V_HEAD_DIM)), KV_LORA_RANK ** -0.5),
        "k_nope_norm_g": gain((QK_NOPE_DIM,)),
        "k_rope_norm_g": gain((QK_ROPE_DIM,)),
        "mla_w_dq": nrm((NB, D, Q_LORA_RANK), D ** -0.5),
        "mla_q_norm_g": gain((NB, Q_LORA_RANK)),
        "mla_w_uq": nrm((NB, Q_LORA_RANK, N_HEADS * (QK_NOPE_DIM + QK_ROPE_DIM)), Q_LORA_RANK ** -0.5),
        "mla_q_nope_norm_g": gain((NB, QK_NOPE_DIM)),
        "mla_q_rope_norm_g": gain((NB, QK_ROPE_DIM)),
        "mla_w_o": nrm((NB, N_HEADS * V_HEAD_DIM, D), (N_HEADS * V_HEAD_DIM) ** -0.5),
    }
    return inputs

def first_block(x, c, positions, ada_w, ada_b, norm1_g, norm2_g, ffn_w_gate, ffn_w_up, ffn_w_down,
              s5_lam_re, s5_lam_im, s5_log_dt, s5_b_re, s5_b_im, s5_c_re, s5_c_im, s5_d, s5_w_glu, s5_b_glu,
              kv_ada_w, kv_ada_b, kv_norm_g, w_kv_a, kv_a_norm_g, w_kv_b, k_nope_norm_g, k_rope_norm_g,
              mla_w_dq, mla_q_norm_g, mla_w_uq, mla_q_nope_norm_g, mla_q_rope_norm_g, mla_w_o):
    cos, sin = rope_cos_sin(positions)
    c_act = jax.nn.silu(c)
    k_nope = k_rope = v = None
    for l in range(DEPTH):
        shift1, scale1, gate1, shift2, scale2, gate2 = jnp.split(c_act @ ada_w[l] + ada_b[l], 6, axis=-1)
        if l == N_A_LAYERS:
            k_shift, k_scale = jnp.split(c_act @ kv_ada_w + kv_ada_b, 2, axis=-1)
            hk = modulate(rms_norm(x, kv_norm_g), k_shift, k_scale)
            k_nope, k_rope, v = shared_mla_kv(hk, cos, sin, w_kv_a, kv_a_norm_g, w_kv_b,
                                              k_nope_norm_g, k_rope_norm_g)
        h = modulate(rms_norm(x, norm1_g[l]), shift1, scale1)
        if l < N_A_LAYERS:
            mix = s5_mixer(h, s5_lam_re[l], s5_lam_im[l], s5_log_dt[l], s5_b_re[l], s5_b_im[l],
                           s5_c_re[l], s5_c_im[l], s5_d[l], s5_w_glu[l], s5_b_glu[l])
        else:
            j = l - N_A_LAYERS
            mix = mla_attention(h, cos, sin, k_nope, k_rope, v, mla_w_dq[j], mla_q_norm_g[j], mla_w_uq[j],
                                mla_q_nope_norm_g[j], mla_q_rope_norm_g[j], mla_w_o[j])
        x = x + gate1[:, None, :] * mix
        h = modulate(rms_norm(x, norm2_g[l]), shift2, scale2)
        x = x + gate2[:, None, :] * swiglu(h, ffn_w_gate[l], ffn_w_up[l], ffn_w_down[l])
    return x


DEPTH_2 = 1

N_META = 16
BLOCK_Q = 128
META_PAD = BLOCK_Q - N_META
ATTN_HEADS = 8
HEAD_DIM = 64
ATTN_WIDTH = ATTN_HEADS * HEAD_DIM
CONV_GROUPS = 8
CONV_WIDTH = 512
CONV_K = 3
D_FF_2 = 2816
NORM_EPS = 1e-6
IN_SPLITS = (ATTN_WIDTH, ATTN_WIDTH, ATTN_WIDTH, ATTN_HEADS,
             CONV_WIDTH, CONV_WIDTH, CONV_WIDTH, D_MODEL, D_MODEL)
IN_COLS = ATTN_WIDTH * 3 + ATTN_HEADS + CONV_WIDTH * 3 + D_MODEL * 2


def rms_norm_2(x, g):
    xf = x.astype(jnp.float32)
    y = xf * lax.rsqrt(jnp.mean(xf * xf, axis=-1, keepdims=True) + NORM_EPS)
    return (y * g.astype(jnp.float32)).astype(x.dtype)

def swiglu_2(x, w_in, w_out):
    a, b = jnp.split(x @ w_in, 2, axis=-1)
    return (jax.nn.silu(a) * b) @ w_out

def split_cols(z):
    idx, acc = [], 0
    for s in IN_SPLITS[:-1]:
        acc += s
        idx.append(acc)
    return jnp.split(z, idx, axis=-1)

def forgetting_attention(q, k, v, log_f):
    B, L, H, Dh = q.shape
    F = jnp.cumsum(log_f, axis=1)
    n_blocks = (L + META_PAD) // BLOCK_Q
    q_blocks = jnp.pad(q, ((0, 0), (META_PAD, 0), (0, 0), (0, 0)))
    q_blocks = q_blocks.reshape(B, n_blocks, BLOCK_Q, H, Dh).transpose(1, 0, 2, 3, 4)
    fq_blocks = jnp.pad(F, ((0, 0), (META_PAD, 0), (0, 0)))
    fq_blocks = fq_blocks.reshape(B, n_blocks, BLOCK_Q, H).transpose(1, 0, 3, 2)
    f_k = F.transpose(0, 2, 1)
    k_pos = jnp.arange(L)
    scale = HEAD_DIM ** -0.5

    def one_block(args):
        blk, qb, fqb = args
        q_pos = blk * BLOCK_Q + jnp.arange(BLOCK_Q) - META_PAD
        s = jnp.einsum('bqhd,bkhd->bhqk', qb, k).astype(jnp.float32) * scale
        s = s + fqb[..., None] - f_k[:, :, None, :]
        mask = k_pos[None, :] <= jnp.maximum(q_pos, 0)[:, None]
        s = jnp.where(mask[None, None], s, -jnp.inf)
        p = jax.nn.softmax(s, axis=-1).astype(v.dtype)
        return jnp.einsum('bhqk,bkhd->bqhd', p, v)

    out = lax.map(one_block, (jnp.arange(n_blocks), q_blocks, fq_blocks))
    out = out.transpose(1, 0, 2, 3, 4).reshape(B, n_blocks * BLOCK_Q, H, Dh)
    return out[:, META_PAD:]

def short_conv(u, w):
    L = u.shape[1]
    up = jnp.pad(u, ((0, 0), (CONV_K - 1, 0), (0, 0)))
    y = up[:, 0:L] * w[0]
    for j in range(1, CONV_K):
        y = y + up[:, j:j + L] * w[j]
    return y

def hybrid_layer(h, w_in, b_forget, conv_w, w_attn_branch, w_conv_branch, w_out,
                 g_ffn1_pre, g_ffn1_post, w_ffn1_in, w_ffn1_out,
                 g_mix_pre, g_mix_post, g_ffn2_pre, g_ffn2_post, w_ffn2_in, w_ffn2_out):
    B, L, _ = h.shape
    h = h + 0.5 * rms_norm_2(swiglu_2(rms_norm_2(h, g_ffn1_pre), w_ffn1_in, w_ffn1_out), g_ffn1_post)
    u = rms_norm_2(h, g_mix_pre)
    q, k, v, f_logit, c_b, c_c, c_in, gate_a, gate_c = split_cols(u @ w_in)
    q = q.reshape(B, L, ATTN_HEADS, HEAD_DIM)
    k = k.reshape(B, L, ATTN_HEADS, HEAD_DIM)
    v = v.reshape(B, L, ATTN_HEADS, HEAD_DIM)
    log_f = jax.nn.log_sigmoid((f_logit + b_forget).astype(jnp.float32))
    y_attn = forgetting_attention(q, k, v, log_f).reshape(B, L, ATTN_WIDTH) @ w_attn_branch
    y_conv = (c_b * short_conv(c_c * c_in, conv_w)) @ w_conv_branch
    mixed = (jax.nn.sigmoid(gate_a) * y_attn + jax.nn.sigmoid(gate_c) * y_conv) @ w_out
    h = h + rms_norm_2(mixed, g_mix_post)
    h = h + 0.5 * rms_norm_2(swiglu_2(rms_norm_2(h, g_ffn2_pre), w_ffn2_in, w_ffn2_out), g_ffn2_post)
    return h

def second_inputs(seed: int = 0) -> dict:
    key = jax.random.key(seed)
    ks = jax.random.split(key, 24)
    nrm = lambda k, shape, scale: jax.random.normal(k, shape, jnp.float32) * scale
    gain = lambda k: 1.0 + 0.05 * jax.random.normal(k, (DEPTH_2, D_MODEL), jnp.float32)
    return {
        "x": nrm(ks[0], (BATCH, SEQ, D_MODEL), 1.0),
        "meta_tokens": nrm(ks[1], (N_META, D_MODEL), 1.0),
        "w_in": nrm(ks[2], (DEPTH_2, D_MODEL, IN_COLS), D_MODEL ** -0.5),
        "b_forget": nrm(ks[3], (DEPTH_2, ATTN_HEADS), 0.1),
        "conv_w": nrm(ks[4], (DEPTH_2, CONV_K, CONV_WIDTH), CONV_K ** -0.5),
        "w_attn_branch": nrm(ks[5], (DEPTH_2, ATTN_WIDTH, D_MODEL), ATTN_WIDTH ** -0.5),
        "w_conv_branch": nrm(ks[6], (DEPTH_2, CONV_WIDTH, D_MODEL), CONV_WIDTH ** -0.5),
        "w_out": nrm(ks[7], (DEPTH_2, D_MODEL, D_MODEL), D_MODEL ** -0.5),
        "g_ffn1_pre": gain(ks[8]),
        "g_ffn1_post": gain(ks[9]),
        "w_ffn1_in": nrm(ks[10], (DEPTH_2, D_MODEL, 2 * D_FF_2), D_MODEL ** -0.5),
        "w_ffn1_out": nrm(ks[11], (DEPTH_2, D_FF_2, D_MODEL), D_FF_2 ** -0.5),
        "g_mix_pre": gain(ks[12]),
        "g_mix_post": gain(ks[13]),
        "g_ffn2_pre": gain(ks[14]),
        "g_ffn2_post": gain(ks[15]),
        "w_ffn2_in": nrm(ks[16], (DEPTH_2, D_MODEL, 2 * D_FF_2), D_MODEL ** -0.5),
        "w_ffn2_out": nrm(ks[17], (DEPTH_2, D_FF_2, D_MODEL), D_FF_2 ** -0.5),
    }

def second_block(x, meta_tokens, w_in, b_forget, conv_w, w_attn_branch, w_conv_branch, w_out,
              g_ffn1_pre, g_ffn1_post, w_ffn1_in, w_ffn1_out,
              g_mix_pre, g_mix_post, g_ffn2_pre, g_ffn2_post, w_ffn2_in, w_ffn2_out):
    B = x.shape[0]
    meta = jnp.broadcast_to(meta_tokens.astype(x.dtype)[None], (B, N_META, x.shape[-1]))
    h = jnp.concatenate([meta, x], axis=1)
    for l in range(DEPTH_2):
        h = hybrid_layer(h, w_in[l], b_forget[l], conv_w[l], w_attn_branch[l], w_conv_branch[l], w_out[l],
                         g_ffn1_pre[l], g_ffn1_post[l], w_ffn1_in[l], w_ffn1_out[l],
                         g_mix_pre[l], g_mix_post[l], g_ffn2_pre[l], g_ffn2_post[l],
                         w_ffn2_in[l], w_ffn2_out[l])
    return h[:, N_META:]


def setup_inputs(seed=0):
    out = dict(first_inputs(seed))
    for name, value in second_inputs(seed + 1).items():
        if name != "x":
            out[name + "_2"] = value
    return out


def reference(
    x, c, positions, ada_w, ada_b, norm1_g, norm2_g, ffn_w_gate, ffn_w_up, ffn_w_down,
    s5_lam_re, s5_lam_im, s5_log_dt, s5_b_re, s5_b_im, s5_c_re, s5_c_im, s5_d, s5_w_glu,
    s5_b_glu, kv_ada_w, kv_ada_b, kv_norm_g, w_kv_a, kv_a_norm_g, w_kv_b, k_nope_norm_g,
    k_rope_norm_g, mla_w_dq, mla_q_norm_g, mla_w_uq, mla_q_nope_norm_g, mla_q_rope_norm_g,
    mla_w_o, meta_tokens_2, w_in_2, b_forget_2, conv_w_2, w_attn_branch_2, w_conv_branch_2,
    w_out_2, g_ffn1_pre_2, g_ffn1_post_2, w_ffn1_in_2, w_ffn1_out_2, g_mix_pre_2, g_mix_post_2,
    g_ffn2_pre_2, g_ffn2_post_2, w_ffn2_in_2, w_ffn2_out_2,
):
    x = first_block(
        x, c, positions, ada_w, ada_b, norm1_g, norm2_g, ffn_w_gate, ffn_w_up, ffn_w_down,
        s5_lam_re, s5_lam_im, s5_log_dt, s5_b_re, s5_b_im, s5_c_re, s5_c_im, s5_d, s5_w_glu,
        s5_b_glu, kv_ada_w, kv_ada_b, kv_norm_g, w_kv_a, kv_a_norm_g, w_kv_b, k_nope_norm_g,
        k_rope_norm_g, mla_w_dq, mla_q_norm_g, mla_w_uq, mla_q_nope_norm_g, mla_q_rope_norm_g,
        mla_w_o,
    )
    return second_block(
        x, meta_tokens_2, w_in_2, b_forget_2, conv_w_2, w_attn_branch_2, w_conv_branch_2,
        w_out_2, g_ffn1_pre_2, g_ffn1_post_2, w_ffn1_in_2, w_ffn1_out_2, g_mix_pre_2,
        g_mix_post_2, g_ffn2_pre_2, g_ffn2_post_2, w_ffn2_in_2, w_ffn2_out_2,
    )


_drawn_inputs = setup_inputs


def setup_inputs(seed=0):
    import zlib

    import numpy as np

    out = dict(_drawn_inputs(seed))
    spreads = {}
    factors = {'norm1_g': 8.0,
     'norm2_g': 4.294,
     's5_lam_re': 200.0,
     's5_log_dt': 2.708,
     's5_b_re': 3.537,
     's5_b_im': 3.44,
     's5_c_re': 3.438,
     's5_c_im': 3.49,
     's5_b_glu': 8.0,
     'kv_ada_b': 6.524,
     'kv_norm_g': 8.0,
     'kv_a_norm_g': 8.0,
     'k_nope_norm_g': 8.0,
     'k_rope_norm_g': 8.0,
     'mla_q_norm_g': 8.0,
     'mla_q_nope_norm_g': 8.0,
     'mla_q_rope_norm_g': 8.0,
     'b_forget_2': 95.088,
     'g_ffn2_post_2': 16.714,
     'meta_tokens_2': 6.545,
     'g_ffn1_pre_2': 8.0,
     'g_ffn1_post_2': 8.0,
     'g_mix_pre_2': 4.634,
     'g_mix_post_2': 7.512,
     'g_ffn2_pre_2': 3.071}
    for name, (base, spread) in spreads.items():
        noise = np.random.default_rng([zlib.crc32(name.encode()), seed]).standard_normal(out[name].shape)
        drawn = base * np.exp(spread * noise) if base else spread * noise
        out[name] = __import__('jax').numpy.asarray(drawn.astype(out[name].dtype))
    for name, factor in factors.items():
        out[name] = (out[name] * factor).astype(out[name].dtype)
    return out
```

```python
import math
import numpy as np
import concourse.bass as bass
from concourse import mybir
from contextlib import ExitStack

D = 1024
SEQ = 256
NMETA = 16
TALL = SEQ + NMETA
F = 2816
P = 128
KT = D // P
FT = F // P
EPS = 1e-6
HEADS1, NOPE, ROPE, VDIM = 16, 64, 32, 64
QK1 = NOPE + ROPE
HEADS2, DH2 = 8, 64
GROUPS, GCH, NST = 64, 16, 64
PAIRS = GROUPS // 2
CW = 512
SCALE1 = 1.0 / math.sqrt(QK1)
SCALE2 = DH2 ** -0.5
QT2 = ((128, 128), (128, 256), (16, 272))
NEG = -1e30
MAGIC = 1.5 * 2.0 ** 23
MAGIC14 = 1.5 * 2.0 ** 9
TWO_PI = 2.0 * math.pi
C1 = 6.28125
C2 = float(np.float32(np.round((TWO_PI - C1) * 2 ** 22) / 2 ** 22))
C3 = TWO_PI - C1 - C2
PI_IN = 3.1415925
SLOTS = 4
SLOTF = FT // 2 * 256

C_ID, C_ONE1024, C_ONE256, C_BLK, C_ROT, C_TRI, C_MASK, C_T = 0, 128, 256, 384, 512, 640, 768, 1152
C_INV, C_EPS, C_HPI, C_ONE, C_SEL, C_END = 1408, 1409, 1410, 1411, 1412, 1413


def constants():
    c = np.zeros((P, C_END), np.float32)
    c[:, C_ID:C_ID + P] = np.eye(P)
    c[:, C_ONE1024:C_ONE1024 + P] = 1.0 / D
    c[:, C_ONE256:C_ONE256 + P] = 1.0 / 256
    c[0:NOPE, C_BLK:C_BLK + NOPE] = 1.0 / NOPE
    c[NOPE:QK1, C_BLK + NOPE:C_BLK + QK1] = 1.0 / ROPE
    for j in range(ROPE // 2):
        c[NOPE + ROPE // 2 + j, C_ROT + NOPE + j] = -1.0
        c[NOPE + j, C_ROT + NOPE + ROPE // 2 + j] = 1.0
    r = np.arange(P)
    c[:, C_TRI:C_TRI + P] = np.where(r[None, :] <= r[:, None], 0.0, NEG)
    half = (r[:, None] < 64) & (r[None, :] >= 64)
    c[:, C_MASK:C_MASK + P] = np.where(half, NEG, 0.0)
    c[:, C_MASK + 2 * P:C_MASK + 3 * P] = np.where(half, NEG, 0.0)
    c[:, C_T:C_T + SEQ] = np.arange(SEQ)
    inv = 1.0 / (np.float32(10000.0) ** (np.arange(0, ROPE, 2, dtype=np.float32) / np.float32(ROPE)))
    c[NOPE:QK1, C_INV] = np.concatenate([inv, inv])
    c[:, C_EPS] = EPS
    c[:, C_HPI] = math.pi / 2
    c[:, C_ONE] = 1.0
    c[0:P:32, C_SEL] = 1.0
    return c


VROWS = [("ada_b", 96), ("kv_ada_b", 16), ("norm1_g", 16), ("norm2_g", 16), ("s5_d", 8), ("s5_b_glu", 8),
         ("kv_norm_g", 8), ("kv_a_norm_g", 2), ("mla_q_norm_g", 2), ("g_ffn1_pre_2", 8), ("g_ffn1_post_2", 8),
         ("g_mix_pre_2", 8), ("g_mix_post_2", 8), ("g_ffn2_pre_2", 8), ("g_ffn2_post_2", 8), ("conv_w_2", 12)]
VAT, _n = {}, 0
for _name, _rows in VROWS:
    VAT[_name] = _n
    _n += _rows
VAT["q96"], VAT["k96"] = _n, _n + 1
assert VAT["norm1_g"] + 16 == P and _n + 2 <= 2 * P


def build(nc, A, out):
    fp32, i32 = mybir.dt.float32, mybir.dt.int32
    ALU, ACT, AX = mybir.AluOpType, mybir.ActivationFunctionType, mybir.AxisListType
    MUL, ADD, SUB = ALU.mult, ALU.add, ALU.subtract
    ctx = ExitStack()
    with ctx:
        def sb(name, shape, dt=fp32):
            return ctx.enter_context(nc.sbuf_tensor(name, shape, dt))

        def sem(name):
            return ctx.enter_context(nc.semaphore(name))

        X = sb("X", [P, KT, TALL])
        H = sb("H", [P, KT, TALL])
        SQ = sb("SQ", [P, KT, TALL])
        RING = sb("RING", [P, SLOTS, SLOTF])
        CN = sb("CN", [P, C_END])
        VEC = sb("VEC", [P, 256])
        VROW = sb("VROW", [P, 2, P])
        MOD = sb("MOD", [P, 112])
        GS = sb("GS", [P, 5, KT])
        GH = sb("GH", [P, 3, KT])
        STD = sb("STD", [P, 512])
        RSTD = sb("RSTD", [P, TALL])
        SG = sb("SG", [P, 2, 2, TALL])
        CROW = sb("CROW", [KT, P])
        CACT = sb("CACT", [P, KT])
        SMALL = sb("SMALL", [P, 64])
        BF = sb("BF", [HEADS2, 1])
        ARENA = sb("ARENA", [P, 30000])
        PS = ctx.enter_context(nc.psum_tensor("PS", [P, 8, 512], fp32))

        def arena(at, *shape):
            n = 1
            for s in shape:
                n *= s
            v = ARENA[:, at:at + n]
            if len(shape) == 2:
                v = v.rearrange("p (a b) -> p a b", b=shape[1])
            if len(shape) == 3:
                v = v.rearrange("p (a b c) -> p a b c", b=shape[1], c=shape[2])
            return v, at + n

        TAB, at = arena(0, 6, 4, SEQ)
        COS, SIN = TAB[:, 0:3, :, :], TAB[:, 3:6, :, :]
        BT, at = arena(at, 2, KT, P)
        CT, at = arena(at, 3, KT, P)
        LAM, at = arena(at, 6, PAIRS)
        ROWS, at = arena(at, 2, 512)
        WORK = at
        PC2, at = arena(at, 8, 2, SEQ)
        PS2, at = arena(at, 8, 2, SEQ)
        ZC, at = arena(at, 4, 2, SEQ)
        ZS, at = arena(at, 4, 2, SEQ)
        assert at <= 30000
        BRAW, at = arena(WORK, 2, PAIRS, GCH)
        BD, at = arena(at, 2, PAIRS, 32)
        CRAW, at = arena(at, 2, KT, P)
        LROW, at = arena(at, 16, P)
        BTMP, at = arena(at, 2, PAIRS, GCH)
        assert at <= 30000
        XIN = SQ[:, :, :].rearrange("p a b -> p (a b)")[:, 0:2 * D].rearrange("p (a b) -> p a b", b=D)
        QH, at = arena(0, HEADS1, SEQ)
        KH, at = arena(at, HEADS1, SEQ)
        VT, at = arena(at, 2, HEADS1 * VDIM)
        HK, at = arena(at, KT, SEQ)
        OA, at = arena(at, KT, SEQ)
        CKV, at = arena(at, 2, SEQ)
        QA, at = arena(at, 2, SEQ)
        KR, at = arena(at, 3, SEQ)
        COSQ, at = arena(at, SEQ)
        SINQ, at = arena(at, SEQ)
        SQH, at = arena(at, 2, 2 * SEQ)
        SDH, at = arena(at, 2, 2 * SEQ)
        ROT, at = arena(at, 2 * SEQ)
        SM1, at = arena(at, 2, 3 * P)
        PT1, at = arena(at, 2, 3 * P)
        POSF, at = arena(at, 2, SEQ)
        assert at <= 30000
        POSI, at = arena(at, SEQ)
        POSI = POSI.bitcast(i32)
        HID, at = arena(0, FT, TALL)
        HIDP = HID.rearrange("p (j two) t -> p j two t", two=2)
        YB, at = arena(at, KT, TALL)
        Q2, at = arena(at, 4, TALL)
        K2, at = arena(at, 4, TALL)
        V2, at = arena(at, 3, HEADS2 * DH2)
        CB, at = arena(at, 4, TALL)
        CC, at = arena(at, 4, TALL)
        CU, at = arena(at, 4, TALL + 2)
        GAT, at = arena(at, 2 * KT, TALL)
        FROW, at = arena(at, 6, TALL)
        FQ, at = arena(at, 3, HEADS2)
        O2, at = arena(at, 4, TALL)
        FB, at = arena(at, HEADS2, TALL)
        SM2, at = arena(at, 2, 3, TALL)
        PT2, at = arena(at, 2, 432)
        assert at <= 30000, at

        ident = CN[:, C_ID:C_ID + P]
        ones1024 = CN[:, C_ONE1024:C_ONE1024 + P]
        ones256 = CN[:, C_ONE256:C_ONE256 + P]
        blk = CN[:, C_BLK:C_BLK + P]
        rot = CN[:, C_ROT:C_ROT + P]
        eps, hpi, one = CN[:, C_EPS:C_EPS + 1], CN[:, C_HPI:C_HPI + 1], CN[:, C_ONE:C_ONE + 1]

        def vec(name, m):
            return VEC[:, VAT[name] + m:VAT[name] + m + 1]

        def w_view(name, *lead):
            w = A[name]
            for l in lead:
                w = w[l]
            return w.rearrange("(k p) c -> p k c", p=P)

        UNITS = []
        AT = {}

        def stream(label, view, kts, c0, c1, width):
            AT[label] = len(UNITS)
            for c in range(c0, c1, width):
                UNITS.append((view[:, kts[0]:kts[1], c:min(c + width, c1)], kts[1] - kts[0], min(width, c1 - c)))

        def stream_ffn(label, gate, g0, up, u0, down):
            AT[label] = len(UNITS)
            UNITS.extend([("ffn", label, None)] * (FT + 8))
            FFN[label] = (gate, g0, up, u0, down)

        FFN = {}
        stream("ada_early", w_view("ada_w", 0), (0, KT), 0, 2 * D, 256)
        stream("ada_late", w_view("ada_w", 0), (0, KT), 2 * D, 6 * D, 256)
        stream("ada1", w_view("ada_w", 1), (0, KT), 0, 6 * D, 256)
        stream("kv_ada", w_view("kv_ada_w"), (0, KT), 0, 2 * D, 256)
        stream("glu", w_view("s5_w_glu", 0), (0, KT), 0, D, 256)
        stream_ffn("ffn0", w_view("ffn_w_gate", 0), 0, w_view("ffn_w_up", 0), 0, w_view("ffn_w_down", 0))
        stream("kva", w_view("w_kv_a"), (0, KT), 0, 288, 288)
        stream("dq", w_view("mla_w_dq", 0), (0, KT), 0, 256, 256)
        stream("kvb", w_view("w_kv_b"), (0, 2), 0, 2048, 1024)
        stream("uq", w_view("mla_w_uq", 0), (0, 2), 0, 1536, 768)
        stream("wo", w_view("mla_w_o", 0), (0, KT), 0, D, 256)
        stream_ffn("ffn1", w_view("ffn_w_gate", 1), 0, w_view("ffn_w_up", 1), 0, w_view("ffn_w_down", 1))
        w1 = w_view("w_ffn1_in_2", 0)
        stream_ffn("ffn2", w1, 0, w1, F // 256, w_view("w_ffn1_out_2", 0))
        wi = w_view("w_in_2", 0)
        stream("q2", wi, (0, KT), 0, 512, 256)
        stream("k2", wi, (0, KT), 512, 1024, 256)
        stream("v2", wi, (0, KT), 1024, 1536, 256)
        stream("f2", wi, (0, KT), 1536, 1544, 8)
        stream("cin", wi, (0, KT), 1544, 3080, 256)
        stream("gates", wi, (0, KT), 3080, 5128, 256)
        stream("attn_br", w_view("w_attn_branch_2", 0), (0, 4), 0, D, 512)
        stream("conv_br", w_view("w_conv_branch_2", 0), (0, 4), 0, D, 512)
        stream("w_out", w_view("w_out_2", 0), (0, KT), 0, D, 256)
        w2 = w_view("w_ffn2_in_2", 0)
        stream_ffn("ffn3", w2, 0, w2, F // 256, w_view("w_ffn2_out_2", 0))

        def slot(u, kts, cols):
            return RING[:, u % SLOTS, 0:kts * cols].rearrange("p (k c) -> p k c", c=cols)

        w_loaded = [sem(f"w_loaded{s}") for s in range(SLOTS)]
        names = """unit_done rope_used const_loaded x_loaded meta_loaded vrow_zero vrow_loaded c_loaded s5_loaded b_loaded cm_loaded pos_loaded bf_loaded
            tr_ready tr_used lam_ready lam_used bt_ready bt_used ct_ready ct_used bd_ready bd_zero cact_ready cexp_ready lrow_dve lrow_act
            b_terms scan_ready zc_ready zs_ready meta_used row_copied ada_cols turn_sin turn_cos xt_ready res_ready norm_sq norm_stat norm_std norm_scaled h_ready
            ada_used bu_ready bu_used prod_ready v_ready z_ready y_ready ysum_ready gelu_ready sig_ready
            silu_ready hid_ready kv_sq kv_stat kv_std kv_norm kr_rot kr_done hp_proj hp_sq hp_stat hp_std hp_scaled hp_rot hp_done
            v_copied hk_scaled hk_ready s_ready s_sb smax_ready exp_ready prob_ready pt_ready pt_copied o_ready o_copied
            rope_sin rope_ang meta_ready qk_copied v2_copied f_act f_dve f_ready fb_ready fq_ready fb_copied fq_copied
            s2_ready s2_sb s2_max s2_exp s2_prob pt2_ready pt2_copied o2_ready o2_copied
            c_copied u_ready conv_ready gate_ready ya_ready mix_ready mix_part out_tr out_copied stored
            dve_step act_step pool_step""".split()
        S = {n: sem(n) for n in names}


        R_INIT, R_GLU, R_FFN0, R_WO, R_FFN1, R_Y2, R_X2, R_YM, R_XM, R_Y3, R_X3 = range(11)
        NORM_IN = [R_INIT, R_GLU, R_FFN0, R_WO, R_FFN1, R_Y2, R_X2, R_YM, R_XM, R_Y3]
        STAT_BANK = [6, 4, 0, 6, 0, 0, 0, 4, 4, 0]
        N_TOK = [SEQ] * 4 + [TALL] * 6
        FFNS = ["ffn0", "ffn1", "ffn2", "ffn3"]
        FFN_H = [1, 3, 4, 6]
        FFN_OUT = [R_FFN0, R_FFN1, R_Y2, R_Y3]
        MT = FT // 2
        ADA_SHIFT1, ADA_SCALE1, ADA_GATE1, ADA_SHIFT2, ADA_SCALE2, ADA_GATE2 = range(0, 48, 8)
        KV_SHIFT, KV_SCALE = 96, 104

        def x_of(n):
            if n in (5, 7, 9):
                return YB
            return X[:, :, TALL - N_TOK[n]:TALL]

        T_ONE = CN[:, C_T:C_T + SEQ]
        block = ctx.enter_context(nc.Block())

        @block.sync
        def _(sp):
            def take(u, dst, src, iteration=None):
                if u >= SLOTS:
                    sp.wait_ge(S["unit_done"], u - SLOTS + 1 if iteration is None
                               else iteration * 4 + (u - SLOTS + 1))
                sp.dma_start(dst, src).then_inc(w_loaded[u % SLOTS], 16)

            u = 0
            while u < len(UNITS):
                view, kts, cols = UNITS[u]
                if view != "ffn":
                    take(u, slot(u, kts, cols), view)
                    u += 1
                    continue
                gate, g0, up, up0, down = FFN[kts]
                gate, up, down = (w.rearrange("p k (n c) -> p k n c", c=256) for w in (gate, up, down))

                def pair(j, q, i):
                    take(u + 2 * q, slot(u + 2 * q, KT, 256), gate[:, :, j + g0, :], i)
                    take(u + 2 * q + 1, slot(u + 2 * q + 1, KT, 256), up[:, :, j + up0, :], i)

                with sp.Fori(0, MT // 2) as i:
                    for q in range(2):
                        pair(i * 2 + q, q, i)
                pair(MT - 1, MT - 1, None)
                u += 2 * MT
                with sp.Fori(0, 2) as i:
                    for q in range(2):
                        for h in range(2):
                            n = u + 2 * q + h
                            take(n, slot(n, MT, 256), down[:, h * MT:(h + 1) * MT, i * 2 + q, :], i)
                u += 8
            for a in range(2):
                sp.wait_ge(S["out_copied"], 2 * a + 2)
                sp.dma_start(out[0, a * P:(a + 1) * P, :], XIN[:, a, :]).then_inc(S["stored"], 16)
            sp.wait_ge(S["stored"], 32)

        @block.gpsimd
        def _(pool):
            nc.gpsimd.memset(VROW[:, :, :], 0.0).then_inc(S["vrow_zero"], 1)
            nc.gpsimd.memset(BD[:, :, :, :], 0.0).then_inc(S["bd_zero"], 1)
            nc.gpsimd.memset(CT[:, :, :, :], 0.0).then_inc(S["bd_zero"], 1)
            nc.gpsimd.memset(SMALL[:, :], 1.0).then_inc(S["bd_zero"], 1)
            pool.wait_ge(S["vrow_zero"], 1)
            for name, rows in VROWS:
                src = A[name]
                flat = src.rearrange(" ".join("abc"[:len(src.shape)]) + " -> (" + " ".join("abc"[:len(src.shape)]) + ")") \
                    if len(src.shape) > 1 else src
                flat = flat.rearrange("(r c) -> r c", c=P)
                at = VAT[name]
                pool.dma_start(VROW[at % P:at % P + rows, at // P, :], flat).then_inc(S["vrow_loaded"], 16)
            for at, parts in ((VAT["q96"], ("mla_q_nope_norm_g", "mla_q_rope_norm_g")),
                              (VAT["k96"], ("k_nope_norm_g", "k_rope_norm_g"))):
                for name, c0, n in zip(parts, (0, NOPE), (NOPE, ROPE)):
                    src = A[name] if len(A[name].shape) == 2 else A[name].unsqueeze(0)
                    pool.dma_start(VROW[at % P:at % P + 1, 1, c0:c0 + n], src).then_inc(S["vrow_loaded"], 16)
            for i, name in enumerate(("s5_b_re", "s5_b_im")):
                pool.dma_start(BRAW[:, i, :, :], A[name][0].rearrange("(k two) n c -> (two n) k c", two=2))\
                    .then_inc(S["b_loaded"], 16)
            for i, name in enumerate(("s5_c_re", "s5_c_im")):
                for d in range(2):
                    pool.dma_start(CRAW[:, i, :, d * NST:(d + 1) * NST],
                                   A[name][0].rearrange("(k g) c n -> (g c) k n", g=8)).then_inc(S["cm_loaded"], 16)
            f_re, f_im = (LAM[:, k, :].unsqueeze(2).broadcast_to([P, PAIRS, GCH]) for k in (4, 5))
            pool.wait_ge(S["b_loaded"], 32)
            pool.wait_ge(S["bd_zero"], 3)
            pool.wait_ge(S["lam_used"], 1)
            for part, (a, b, op) in enumerate(((0, 1, SUB), (1, 0, ADD))):
                nc.gpsimd.tensor_tensor(BTMP[:, 0, :, :], f_re, BRAW[:, a, :, :], MUL).then_inc(S["b_terms"], 1)
                nc.gpsimd.tensor_tensor(BTMP[:, 1, :, :], f_im, BRAW[:, b, :, :], MUL).then_inc(S["b_terms"], 1)
                pool.wait_ge(S["b_terms"], 2 * part + 2)
                for g in range(2):
                    rows = slice(64 * g, 64 * g + 64)
                    nc.gpsimd.tensor_tensor(BD[rows, part, :, g * GCH:(g + 1) * GCH], BTMP[rows, 0, :, :], BTMP[rows, 1, :, :], op)\
                        .then_inc(S["bd_ready"], 1)
                pool.wait_ge(S["bd_ready"], 2 * part + 2)

            def turned(kt):
                pc, ps = PC2[:, 4 * (kt % 2):4 * (kt % 2) + 4], PS2[:, 4 * (kt % 2):4 * (kt % 2) + 4]
                pool.wait_ge(S["prod_ready"], 2 * kt + 2)
                nc.gpsimd.tensor_tensor(pc[:, :, 0, :], pc[:, :, 0, :], ps[:, :, 1, :], ADD)
                nc.gpsimd.tensor_tensor(pc[:, :, 1, :], pc[:, :, 1, :], ps[:, :, 0, :], SUB).then_inc(S["v_ready"], 1)

            turned(0)
            for kt in range(KT):
                if kt + 1 < KT:
                    turned(kt + 1)
                pool.wait_ge(S["scan_ready"], kt + 1)
                if kt >= 1:
                    pool.wait_ge(S["y_ready"], kt)
                t = SIN[:, kt % 3, :, :].unsqueeze(2).broadcast_to([P, 4, 2, SEQ])
                nc.gpsimd.tensor_tensor(ZS[:, :, :, :], PC2[:, 4 * (kt % 2):4 * (kt % 2) + 4], t, MUL).then_inc(S["zs_ready"], 1)

        @block.scalar
        def _(act):
            steps = [0]

            def link(ins):
                steps[0] += 1
                ins.then_inc(S["act_step"], 1)
                act.wait_ge(S["act_step"], steps[0])

            def squares(n):
                x, T = x_of(n), N_TOK[n]
                for m in range(KT):
                    act.wait_ge(S["res_ready"], KT * NORM_IN[n] + m + 1)
                    nc.scalar.activation(SQ[:, m, 0:T], x[:, m, :], ACT.Square).then_inc(S["norm_sq"], 1)

            def std(n):
                T = N_TOK[n]
                act.wait_ge(S["norm_stat"], n + 1)
                link(nc.scalar.activation(STD[:, 0:T], PS[:, STAT_BANK[n], 0:T], ACT.Ln, bias=eps))
                nc.scalar.activation(RSTD[:, 0:T], STD[:, 0:T], ACT.Exp, scale=-0.5).then_inc(S["norm_std"], 1)

            def shift(n, col):
                for m in range(KT):
                    act.wait_ge(S["norm_scaled"], KT * n + m + 1)
                    nc.scalar.activation(H[:, m, 0:SEQ], H[:, m, 0:SEQ], ACT.Identity,
                                         bias=MOD[:, col + m:col + m + 1]).then_inc(S["h_ready"], 1)

            def silu_ffn(f):
                T, u0, base = (SEQ if f < 2 else TALL), AT[FFNS[f]], MT * f

                def pair(j, p):
                    act.wait_ge(S["unit_done"], j * 2 + (u0 + 2))
                    if not (isinstance(j, int) and j < 2):
                        act.wait_ge(S["hid_ready"], j + (base - 1))
                    nc.scalar.activation(SG[:, p, :, 0:T], PS[:, 4 * p:4 * p + 2, 0:T], ACT.Silu)\
                        .then_inc(S["silu_ready"], 1)

                pair(0, 0)
                pair(1, 1)
                with act.Fori(1, MT // 2) as i:
                    pair(i * 2, 0)
                    pair(i * 2 + 1, 1)
                pair(MT - 1, 0)

            act.dma_start(CN[:, :], A["consts"]).then_inc(S["const_loaded"], 16)
            act.dma_start(XIN[:, :, :], A["x"][0].rearrange("(a p) c -> p a c", p=P)).then_inc(S["x_loaded"], 16)
            act.dma_start(CROW[:, :], A["c"].rearrange("a (k p) -> (a k) p", p=P)).then_inc(S["c_loaded"], 16)
            act.dma_start(LROW[0:PAIRS, 0, :], A["s5_lam_re"][0].rearrange("(k two) n -> k (two n)", two=2)).then_inc(S["s5_loaded"], 16)
            act.dma_start(LROW[0:PAIRS, 1, :], A["s5_lam_im"][0].rearrange("(k two) n -> k (two n)", two=2)).then_inc(S["s5_loaded"], 16)
            act.dma_start(LROW[0:PAIRS, 2, 0:2], A["s5_log_dt"][0].rearrange("(k two) -> k two", two=2)).then_inc(S["s5_loaded"], 16)
            act.dma_start(SG[0:NMETA, :, :, :].rearrange("p a b c -> p (a b c)")[:, 0:D], A["meta_tokens_2"]).then_inc(S["meta_loaded"], 16)
            act.dma_start(BF[:, :], A["b_forget_2"].rearrange("a h -> h a")).then_inc(S["bf_loaded"], 16)
            act.wait_ge(S["cact_ready"], 1)
            nc.scalar.activation(CACT[:, :], PS[:, 5, 0:KT], ACT.Silu).then_inc(S["cexp_ready"], 1)
            squares(0)
            act.wait_ge(S["s5_loaded"], 48)
            nc.scalar.activation(LROW[0:PAIRS, 3, 0:2], LROW[0:PAIRS, 2, 0:2], ACT.Exp).then_inc(S["lrow_act"], 1)
            act.wait_ge(S["lrow_dve"], 1)
            nc.scalar.activation(LROW[0:PAIRS, 6, :], LROW[0:PAIRS, 4, :], ACT.Exp).then_inc(S["lrow_act"], 1)
            act.wait_ge(S["lrow_dve"], 2)
            nc.scalar.activation(LROW[0:PAIRS, 10, :], LROW[0:PAIRS, 8, :], ACT.Sin).then_inc(S["lrow_act"], 1)
            nc.scalar.activation(LROW[0:PAIRS, 11, :], LROW[0:PAIRS, 9, :], ACT.Sin, scale=-1.0, bias=hpi[0:PAIRS])\
                .then_inc(S["lrow_act"], 1)
            std(0)
            def row_copy(s):
                act.wait_ge(S["unit_done"], 2 * s + 2)
                if s >= 2:
                    act.wait_ge(S["ada_cols"], s - 1)
                nc.scalar.copy(ROWS[:, s % 2, :], PS[:, 4, :]).then_inc(S["row_copied"], 1)

            def table(kt):
                act.wait_ge(S["turn_cos"], kt + 1)
                k = kt % 3
                nc.scalar.activation(SIN[:, k, :, :], COS[:, k, :, :], ACT.Sin, scale=2 * PI_IN)
                link(nc.scalar.activation(COS[:, k, :, :], COS[:, k, :, :], ACT.Abs))
                nc.scalar.activation(COS[:, k, :, :], COS[:, k, :, :], ACT.Sin, scale=-TWO_PI, bias=hpi)\
                    .then_inc(S["turn_sin"], 1)

            for s in range(4):
                row_copy(s)
            shift(0, ADA_SHIFT1)
            for s in range(4, 12):
                row_copy(s)
                if s in (7, 9):
                    table((s - 7) // 2)
            for kt in range(KT):
                if kt + 2 < KT:
                    table(kt + 2)
                row_copy(12 + 2 * kt)
                row_copy(13 + 2 * kt)
            for kt in range(KT):
                act.wait_ge(S["ysum_ready"], kt + 1)
                nc.scalar.activation(H[:, kt, 0:SEQ], H[:, kt, 0:SEQ], ACT.Gelu_apprx_tanh).then_inc(S["gelu_ready"], 1)
            for c in range(4):
                act.wait_ge(S["unit_done"], AT["glu"] + c + 1)
                if c >= 2:
                    act.wait_ge(S["res_ready"], KT * R_GLU + 2 * (c - 1))
                for half in range(2):
                    nc.scalar.activation(SG[:, c % 2, half, 0:SEQ], PS[:, 2 * (c % 2) + half, 0:SEQ], ACT.Sigmoid,
                                         bias=vec("s5_b_glu", 2 * c + half)).then_inc(S["sig_ready"], 1)
            squares(1)
            std(1)
            shift(1, ADA_SHIFT2)
            silu_ffn(0)
            squares(2)
            std(2)
            act.dma_start(POSI[NOPE:QK1, :], A["positions"].broadcast_to([ROPE, SEQ])).then_inc(S["pos_loaded"], 16)
            act.wait_ge(S["rope_ang"], 1)
            nc.scalar.activation(SINQ[NOPE:QK1, :], POSF[NOPE:QK1, 0, :], ACT.Sin)
            nc.scalar.activation(COSQ[NOPE:QK1, :], POSF[NOPE:QK1, 1, :], ACT.Sin, scale=-1.0, bias=hpi[NOPE:QK1])\
                .then_inc(S["rope_sin"], 1)
            for m in range(KT):
                act.wait_ge(S["hk_scaled"], m + 1)
                nc.scalar.activation(HK[:, m, :], HK[:, m, :], ACT.Identity, bias=MOD[:, KV_SHIFT + m:KV_SHIFT + m + 1])\
                    .then_inc(S["hk_ready"], 1)
            shift(2, 48 + ADA_SHIFT1)
            act.wait_ge(S["unit_done"], AT["kva"] + 1)
            for b in range(3):
                rows = P if b < 2 else QK1
                nc.scalar.activation(SQ[0:rows, b, 0:SEQ], PS[0:rows, b, 0:SEQ], ACT.Square).then_inc(S["kv_sq"], 1)
            act.wait_ge(S["unit_done"], AT["dq"] + 1)
            for b in range(3, 5):
                nc.scalar.activation(SQ[:, b, 0:SEQ], PS[:, b, 0:SEQ], ACT.Square).then_inc(S["kv_sq"], 1)
            act.wait_ge(S["kv_stat"], 1)
            nc.scalar.activation(STD[:, :], PS[:, 5, :], ACT.Ln, bias=eps)
            link(nc.scalar.activation(SDH[0:QK1, 0, 0:SEQ], PS[0:QK1, 6, 0:SEQ], ACT.Ln, bias=eps[0:QK1]))
            nc.scalar.activation(STD[:, :], STD[:, :], ACT.Exp, scale=-0.5).then_inc(S["kv_std"], 1)
            nc.scalar.activation(SDH[0:QK1, 0, 0:SEQ], SDH[0:QK1, 0, 0:SEQ], ACT.Exp, scale=-0.5).then_inc(S["kv_std"], 1)
            for s in range(17):
                if s < 16:
                    rows = NOPE if s < 8 else QK1
                    if s in (11, 15):
                        act.wait_ge(S["unit_done"], AT["uq"] + (s - 7) // 4)
                    else:
                        act.wait_ge(S["hp_proj"], s + 1 if s < 11 else s)
                    if s >= 2:
                        act.wait_ge(S["hp_stat"], s - 1)
                    nc.scalar.activation(SQH[0:rows, s % 2, :], PS[0:rows, s % 2, :], ACT.Square).then_inc(S["hp_sq"], 1)
                if s in (4, 8):
                    c = s // 4 - 1
                    act.wait_ge(S["unit_done"], AT["kvb"] + c + 1)
                    for tt in range(2):
                        nc.scalar.copy(VT[:, tt, c * 512:(c + 1) * 512], PS[:, 6 + tt, :]).then_inc(S["v_copied"], 1)
                if s >= 1:
                    s1 = s - 1
                    rows = NOPE if s1 < 8 else QK1
                    act.wait_ge(S["hp_stat"], s1 + 1)
                    if s1 >= 2:
                        act.wait_ge(S["hp_scaled"], s1 - 1)
                    if s1 == 0:
                        act.wait_ge(S["kv_norm"], 1)
                    sd = SDH[0:rows, s1 % 2, :]
                    link(nc.scalar.activation(sd, PS[0:rows, 2 + s1 % 2, :], ACT.Ln, bias=eps[0:rows]))
                    nc.scalar.activation(sd, sd, ACT.Exp, scale=-0.5).then_inc(S["hp_std"], 1)
            for h in range(HEADS1 + 2):
                if h < HEADS1:
                    act.wait_ge(S["smax_ready"], h + 1)
                    q, k = SM1[:, h % 2, 0:P], SM1[:, h % 2, P:3 * P]
                    b = 4 * (h % 2)
                    nc.scalar.activation(q, q, ACT.Exp, bias=SMALL[:, b:b + 1], accum_out=SMALL[:, b + 2:b + 3])
                    nc.scalar.activation(k, k, ACT.Exp, bias=SMALL[:, b + 1:b + 2], accum_out=SMALL[:, b + 3:b + 4])\
                        .then_inc(S["exp_ready"], 1)
                if 1 <= h <= HEADS1:
                    g = h - 1
                    act.wait_ge(S["pt_ready"], g + 1)
                    if g >= 2:
                        act.wait_ge(S["o_ready"], g - 1)
                    nc.scalar.copy(PT1[:, g % 2, :], PS[:, 2 + g % 2, 0:3 * P]).then_inc(S["pt_copied"], 1)
                if h >= 2 and h % 2:
                    g = h - 2
                    act.wait_ge(S["o_ready"], g + 1)
                    nc.scalar.copy(OA[:, g // 2, :], PS[:, 4 + g // 2 % 2, 0:SEQ]).then_inc(S["o_copied"], 1)
            squares(3)
            std(3)
            shift(3, 48 + ADA_SHIFT2)
            silu_ffn(1)
            squares(4)
            std(4)
            silu_ffn(2)
            squares(5)
            std(5)
            squares(6)
            std(6)
            for i, (dst, label) in enumerate(((Q2, "q2"), (Q2, "q2"), (K2, "k2"), (K2, "k2"))):
                c = i % 2
                act.wait_ge(S["unit_done"], AT[label] + c + 1)
                nc.scalar.activation(dst[:, 2 * c:2 * c + 2, :], PS[:, 2 * i:2 * i + 2, 0:TALL], ACT.Copy,
                                     scale=SCALE2 if label == "q2" else 1.0).then_inc(S["qk_copied"], 1)
            act.wait_ge(S["unit_done"], AT["v2"] + 2)
            for tt, rows in enumerate((P, P, NMETA)):
                nc.scalar.copy(V2[0:rows, tt, :], PS[0:rows, tt, :]).then_inc(S["v2_copied"], 1)
            act.wait_ge(S["unit_done"], AT["f2"] + 1)
            act.wait_ge(S["bf_loaded"], 16)
            link(nc.scalar.activation(FROW[0:HEADS2, 0, :], PS[0:HEADS2, 3, 0:TALL], ACT.Identity, bias=BF[:, :]))
            link(nc.scalar.activation(FROW[0:HEADS2, 1, :], FROW[0:HEADS2, 0, :], ACT.Abs))
            link(nc.scalar.activation(FROW[0:HEADS2, 2, :], FROW[0:HEADS2, 1, :], ACT.Exp, scale=-1.0))
            nc.scalar.activation(FROW[0:HEADS2, 3, :], FROW[0:HEADS2, 2, :], ACT.Ln, bias=one[0:HEADS2]).then_inc(S["f_act"], 1)
            for i in range(4):
                dst = CB if i < 2 else CC
                act.wait_ge(S["unit_done"], AT["cin"] + i + 1)
                c = i % 2
                nc.scalar.copy(dst[:, 2 * c:2 * c + 2, :], PS[:, 4 + 2 * c:6 + 2 * c, 0:TALL]).then_inc(S["c_copied"], 1)
            for i in range(8):
                act.wait_ge(S["unit_done"], AT["gates"] + i + 1)
                c = i % 2
                nc.scalar.activation(GAT[:, 2 * i:2 * i + 2, :], PS[:, 2 * c:2 * c + 2, 0:TALL], ACT.Sigmoid)\
                    .then_inc(S["gate_ready"], 1)
            for h in range(HEADS2):
                act.wait_ge(S["fb_ready"], h + 1)
                nc.scalar.activation(FB[:, h, :], PS[:, 4 + h % 4, 0:TALL], ACT.Copy, scale=-1.0).then_inc(S["fb_copied"], 1)
            for h in range(HEADS2 + 2):
                if h < HEADS2:
                    act.wait_ge(S["s2_max"], h + 1)
                    b = 16 + 8 * (h % 2)
                    for qt, (rows, keys) in enumerate(QT2):
                        v = SM2[0:rows, h % 2, qt, 0:keys]
                        ins = nc.scalar.activation(v, v, ACT.Exp, bias=SMALL[0:rows, b + qt:b + qt + 1],
                                                   accum_out=SMALL[0:rows, b + 4 + qt:b + 5 + qt])
                    ins.then_inc(S["s2_exp"], 1)
                if 1 <= h <= HEADS2:
                    g = h - 1
                    act.wait_ge(S["pt2_ready"], g + 1)
                    if g >= 2:
                        act.wait_ge(S["o2_ready"], g - 1)
                    nc.scalar.copy(PT2[:, g % 2, 0:416], PS[:, 4 + g % 2, 0:416])
                    nc.scalar.copy(PT2[0:NMETA, g % 2, 416:432], PS[0:NMETA, 4 + g % 2, 416:432]).then_inc(S["pt2_copied"], 1)
                if h >= 2 and h % 2:
                    g = h - 2
                    act.wait_ge(S["o2_ready"], g + 1)
                    nc.scalar.copy(O2[:, g // 2, :], PS[:, 6 + g // 2 % 2, 0:TALL]).then_inc(S["o2_copied"], 1)
            squares(7)
            std(7)
            squares(8)
            std(8)
            silu_ffn(3)
            squares(9)
            std(9)
            for b in range(4):
                act.wait_ge(S["out_tr"], b + 1)
                nc.scalar.copy(XIN[:, b // 2, (b % 2) * 512:(b % 2) * 512 + 512], PS[:, b, :]).then_inc(S["out_copied"], 1)

        @block.vector
        def _(dve):
            steps = [0]

            def link(ins):
                steps[0] += 1
                ins.then_inc(S["dve_step"], 1)
                dve.wait_ge(S["dve_step"], steps[0])

            V = nc.vector

            def rstd(n):
                dve.wait_ge(S["norm_std"], n + 1)

            def scaled(n, gains, dst, done):
                x, T = x_of(n), N_TOK[n]
                for m in range(KT):
                    V.scalar_tensor_tensor(dst[:, m, 0:T], x[:, m, :], gains[:, m:m + 1], RSTD[:, 0:T], MUL, MUL)\
                        .then_inc(S[done], 1)

            def ffn(f):
                T, u0, base = (SEQ if f < 2 else TALL), AT[FFNS[f]], MT * f

                def pair(j, p):
                    dve.wait_ge(S["silu_ready"], j + (base + 1))
                    V.tensor_tensor(HIDP[:, j, :, 0:T], SG[:, p, :, 0:T], PS[:, 4 * p + 2:4 * p + 4, 0:T], MUL)\
                        .then_inc(S["hid_ready"], 1)

                with dve.Fori(0, MT // 2) as i:
                    pair(i * 2, 0)
                    pair(i * 2 + 1, 1)
                pair(MT - 1, 0)

            def down_used(f, gate_col=None):
                u0 = AT[FFNS[f]] + 2 * MT
                for m in range(KT):
                    if m % 2 == 0:
                        dve.wait_ge(S["unit_done"], u0 + m + 2)
                    y = PS[:, 4 + m % 4, 0:(SEQ if f < 2 else TALL)]
                    if gate_col is None:
                        V.tensor_copy(YB[:, m, :], y).then_inc(S["res_ready"], 1)
                    else:
                        V.scalar_tensor_tensor(X[:, m, NMETA:], y, MOD[:, gate_col + m:gate_col + m + 1],
                                               X[:, m, NMETA:], MUL, ADD).then_inc(S["res_ready"], 1)

            def post(n, k):
                rstd(n)
                for m in range(KT):
                    ins = V.scalar_tensor_tensor(YB[:, m, :], YB[:, m, :], GH[:, k, m:m + 1], RSTD[:, :], MUL, MUL)
                link(ins)
                for m in range(KT):
                    V.tensor_tensor(X[:, m, :], X[:, m, :], YB[:, m, :], ADD).then_inc(S["res_ready"], 1)

            for b in range(4):
                dve.wait_ge(S["xt_ready"], b + 1)
                V.tensor_copy(X[:, 2 * b:2 * b + 2, NMETA:], PS[:, b, :].rearrange("p (m t) -> p m t", m=2)).then_inc(S["res_ready"], 2)
            dve.wait_ge(S["tr_ready"], 1)
            V.tensor_copy(VEC[:, :], PS[:, 7, 0:256]).then_inc(S["tr_used"], 1)
            dve.wait_ge(S["meta_ready"], 1)
            V.tensor_copy(X[:, :, 0:NMETA], PS[:, 4, 0:KT * NMETA].rearrange("p (m t) -> p m t", m=KT)).then_inc(S["meta_used"], 1)
            L = [LROW[0:PAIRS, r, :] for r in range(16)]
            dt = LROW[0:PAIRS, 3, 0:2].unsqueeze(2).broadcast_to([PAIRS, 2, NST])

            def by_dt(r):
                return LROW[0:PAIRS, r, :].rearrange("p (g n) -> p g n", g=2)

            dve.wait_ge(S["lrow_act"], 1)
            V.tensor_tensor(by_dt(4), by_dt(0), dt, MUL).then_inc(S["lrow_dve"], 1)
            link(V.tensor_tensor(by_dt(5), by_dt(1), dt, MUL))
            link(V.tensor_scalar(L[7], L[5], 1.0 / TWO_PI, MAGIC, MUL, ADD))
            link(V.tensor_scalar(L[7], L[7], MAGIC, None, SUB))
            link(V.scalar_tensor_tensor(L[8], L[7], -C1, L[5], MUL, ADD))
            link(V.scalar_tensor_tensor(L[8], L[7], -C2, L[8], MUL, ADD))
            link(V.scalar_tensor_tensor(L[8], L[7], -C3, L[8], MUL, ADD))
            link(V.tensor_scalar(L[8], L[8], PI_IN, -PI_IN, ALU.min, ALU.max))
            V.scalar_tensor_tensor(L[9], L[8], -1.0, L[8], MUL, ALU.max).then_inc(S["lrow_dve"], 1)
            link(V.tensor_tensor(L[14], L[0], L[0], MUL))
            link(V.tensor_tensor(L[15], L[1], L[1], MUL))
            link(V.tensor_tensor(L[14], L[14], L[15], ADD))
            link(V.reciprocal(L[14], L[14]))
            dve.wait_ge(S["lrow_act"], 4)
            V.tensor_tensor(L[12], L[6], L[11], MUL)
            link(V.tensor_tensor(L[13], L[6], L[10], MUL))
            link(V.tensor_scalar(L[12], L[12], 1.0, None, SUB))
            V.tensor_tensor(L[15], L[12], L[0], MUL)
            link(V.tensor_tensor(L[5], L[13], L[1], MUL))
            link(V.tensor_tensor(L[15], L[15], L[5], ADD))
            link(V.tensor_tensor(L[15], L[15], L[14], MUL))
            V.tensor_tensor(L[5], L[13], L[0], MUL)
            link(V.tensor_tensor(L[4], L[12], L[1], MUL))
            link(V.tensor_tensor(L[5], L[5], L[4], SUB))
            link(V.tensor_tensor(L[5], L[5], L[14], MUL))
            link(V.tensor_scalar(L[7], L[8], 1.0 / TWO_PI, None, MUL))
            link(V.tensor_scalar(L[9], L[7], MAGIC14, MAGIC14, ADD, SUB))
            V.tensor_tensor(L[11], L[7], L[9], SUB).then_inc(S["lrow_dve"], 1)
            def modulation(c0, c1):
                link(V.tensor_tensor(MOD[:, c0:c1], PS[:, 7, c0:c1], VEC[:, c0:c1], ADD))

            def gain(k, col, g):
                return V.scalar_tensor_tensor(GS[:, k, :], MOD[:, col:col + KT], 1.0, VEC[:, g:g + KT], ADD, MUL)

            dve.wait_ge(S["ada_cols"], 4)
            modulation(0, 16)
            gain(0, ADA_SCALE1, VAT["norm1_g"]).then_inc(S["ada_used"], 1)
            dve.wait_ge(S["ada_used"], 1)
            rstd(0)
            scaled(0, GS[:, 0, :], H, "norm_scaled")
            dve.wait_ge(S["bd_zero"], 3)
            dve.wait_ge(S["lam_ready"], 1)
            V.tensor_copy(LAM[:, :, :], PS[:, 6, 0:6 * PAIRS].rearrange("p (a b) -> p a b", b=PAIRS)).then_inc(S["lam_used"], 1)
            dve.wait_ge(S["lam_used"], 1)
            dve.wait_ge(S["ct_ready"], 1)
            for i, (b, sign) in enumerate(((0, 1.0), (0, -1.0), (2, -1.0))):
                for g in range(2):
                    rows = slice(64 * g, 64 * g + 64)
                    src = PS[rows, b:b + 2, :].rearrange("p b (q g c) -> p (b q) g c", g=2, c=GCH)[:, :, g, :]
                    dst = CT[rows, i, :, :].rearrange("p k (q g c) -> p (k q) g c", g=2, c=GCH)[:, :, g, :]
                    ins = V.tensor_scalar(dst, src, sign, None, MUL)
            ins.then_inc(S["ct_used"], 1)

            def turns(kt):
                m, f = SIN[:, kt % 3, :, :], COS[:, kt % 3, :, :]
                lam = [[LAM[:, k, 4 * kt + q:4 * kt + q + 1] for q in range(4)] for k in range(4)]
                for q in range(4):
                    ins = V.tensor_scalar(m[:, q, :], T_ONE, lam[1][q], MAGIC, MUL, ADD)
                link(ins)
                link(V.tensor_scalar(m, m, MAGIC, None, SUB))
                for q in range(4):
                    ins = V.scalar_tensor_tensor(f[:, q, :], T_ONE, lam[2][q], m[:, q, :], MUL, SUB)
                link(ins)
                for q in range(4):
                    ins = V.scalar_tensor_tensor(f[:, q, :], T_ONE, lam[3][q], f[:, q, :], MUL, ADD)
                link(ins)
                V.tensor_scalar(f, f, 0.5, -0.5, ALU.min, ALU.max).then_inc(S["turn_cos"], 1)

            turns(0)
            dve.wait_ge(S["bt_ready"], 1)
            for part in range(2):
                ins = V.tensor_copy(BT[:, part, :, :].rearrange("p k c -> p (k c)"),
                                    PS[:, 2 * part:2 * part + 2, :].rearrange("p b c -> p (b c)"))
            ins.then_inc(S["bt_used"], 1)
            turns(1)

            def turned_in(kt):
                dve.wait_ge(S["turn_sin"], kt + 1)
                dve.wait_ge(S["bu_ready"], kt + 1)
                if kt >= 2:
                    dve.wait_ge(S["zs_ready"], kt - 1)
                bu = PS[:, 0:4, :].rearrange("p q (a t) -> p q a t", a=2)
                for tab, dst in ((COS, PC2), (SIN, PS2)):
                    t = tab[:, kt % 3, :, :].unsqueeze(2).broadcast_to([P, 4, 2, SEQ])
                    V.tensor_tensor(dst[:, 4 * (kt % 2):4 * (kt % 2) + 4], bu, t, MUL).then_inc(S["prod_ready"], 1)

            def y_sum(kt):
                dve.wait_ge(S["y_ready"], kt + 1)
                V.scalar_tensor_tensor(H[:, kt, 0:SEQ], H[:, kt, 0:SEQ], vec("s5_d", kt), PS[:, 5 + kt % 2, 0:SEQ], MUL, ADD)\
                    .then_inc(S["ysum_ready"], 1)

            turned_in(0)
            for kt in range(KT):
                if kt + 1 < KT:
                    turned_in(kt + 1)
                dve.wait_ge(S["v_ready"], kt + 1)
                z = PC2[:, 4 * (kt % 2):4 * (kt % 2) + 4]
                for q in range(4):
                    r = LAM[:, 0, 4 * kt + q:4 * kt + q + 1].broadcast_to([P, SEQ])
                    for a in range(2):
                        ins = V.tensor_tensor_scan(z[:, q, a, :], r, z[:, q, a, :], 0.0, MUL, ADD)
                ins.then_inc(S["scan_ready"], 1)
                dve.wait_ge(S["scan_ready"], kt + 1)
                if kt >= 1:
                    dve.wait_ge(S["y_ready"], kt)
                t = COS[:, kt % 3, :, :].unsqueeze(2).broadcast_to([P, 4, 2, SEQ])
                V.tensor_tensor(ZC[:, :, :, :], z, t, MUL).then_inc(S["zc_ready"], 1)
                if kt + 2 < KT:
                    if kt >= 1:
                        dve.wait_ge(S["zs_ready"], kt)
                    turns(kt + 2)
                if kt >= 1:
                    y_sum(kt - 1)
            y_sum(KT - 1)
            dve.wait_ge(S["ada_cols"], 28)
            modulation(16, 112)
            gain(1, ADA_SCALE2, VAT["norm2_g"])
            gain(2, 48 + ADA_SCALE1, VAT["norm1_g"] + KT)
            gain(3, 48 + ADA_SCALE2, VAT["norm2_g"] + KT)
            gain(4, KV_SCALE, VAT["kv_norm_g"])
            for k, (name, c) in enumerate((("g_ffn1_post_2", 0.5), ("g_mix_post_2", 1.0), ("g_ffn2_post_2", 0.5))):
                ins = V.tensor_scalar(GH[:, k, :], VEC[:, VAT[name]:VAT[name] + KT], c, None, MUL)
            link(ins)
            for m in range(KT):
                dve.wait_ge(S["sig_ready"], m + 1)
                v = SG[:, m // 2 % 2, m % 2, 0:SEQ]
                link(V.tensor_tensor(v, v, H[:, m, 0:SEQ], MUL))
                V.scalar_tensor_tensor(X[:, m, NMETA:], v, MOD[:, ADA_GATE1 + m:ADA_GATE1 + m + 1], X[:, m, NMETA:], MUL, ADD)\
                    .then_inc(S["res_ready"], 1)
            rstd(1)
            scaled(1, GS[:, 1, :], H, "norm_scaled")
            ffn(0)
            down_used(0, ADA_GATE2)
            dve.wait_ge(S["pos_loaded"], 16)
            R = slice(NOPE, QK1)
            link(V.tensor_copy(POSF[R, 0, :], POSI[R, :]))
            link(V.tensor_scalar(POSF[R, 0, :], POSF[R, 0, :], CN[R, C_INV:C_INV + 1], None, MUL))
            link(V.tensor_scalar(POSF[R, 1, :], POSF[R, 0, :], 1.0 / TWO_PI, MAGIC, MUL, ADD))
            link(V.tensor_scalar(POSF[R, 1, :], POSF[R, 1, :], MAGIC, None, SUB))
            for c in (C1, C2, C3):
                link(V.scalar_tensor_tensor(POSF[R, 0, :], POSF[R, 1, :], -c, POSF[R, 0, :], MUL, ADD))
            link(V.tensor_scalar(POSF[R, 0, :], POSF[R, 0, :], PI_IN, -PI_IN, ALU.min, ALU.max))
            V.scalar_tensor_tensor(POSF[R, 1, :], POSF[R, 0, :], -1.0, POSF[R, 0, :], MUL, ALU.max).then_inc(S["rope_ang"], 1)
            rstd(2)
            scaled(2, GS[:, 4, :], HK, "hk_scaled")
            scaled(2, GS[:, 2, :], H, "norm_scaled")
            dve.wait_ge(S["kv_std"], 2)
            for i in range(2):
                V.scalar_tensor_tensor(CKV[:, i, :], PS[:, i, 0:SEQ], vec("kv_a_norm_g", i), STD[:, 0:SEQ], MUL, MUL)
                V.scalar_tensor_tensor(QA[:, i, :], PS[:, 3 + i, 0:SEQ], vec("mla_q_norm_g", i), STD[:, SEQ:], MUL, MUL)
            V.scalar_tensor_tensor(KR[0:QK1, 0, :], PS[0:QK1, 2, 0:SEQ], VEC[0:QK1, VAT["k96"]:VAT["k96"] + 1],
                                   SDH[0:QK1, 0, 0:SEQ], MUL, MUL).then_inc(S["kv_norm"], 1)
            dve.wait_ge(S["rope_sin"], 1)
            dve.wait_ge(S["kr_rot"], 1)
            V.tensor_tensor(KR[R, 1, :], PS[R, 7, 0:SEQ], SINQ[R, :], MUL)
            link(V.tensor_tensor(KR[R, 2, :], KR[R, 0, :], COSQ[R, :], MUL))
            link(V.tensor_tensor(KR[R, 1, :], KR[R, 1, :], KR[R, 2, :], ADD))
            V.tensor_copy(KH[R, :, :], KR[R, 1, :].unsqueeze(1).broadcast_to([ROPE, HEADS1, SEQ])).then_inc(S["kr_done"], 1)

            def two(ap):
                return ap.rearrange("p a t -> p (a t)")

            for s in range(17):
                if s < 16:
                    rows, dst, g = (NOPE, KH, VAT["k96"]) if s < 8 else (QK1, QH, VAT["q96"])
                    h = 2 * (s % 8)
                    dve.wait_ge(S["hp_std"], s + 1)
                    sd = SDH[0:rows, s % 2, :]
                    V.scalar_tensor_tensor(two(dst[0:rows, h:h + 2, :]), PS[0:rows, s % 2, :], VEC[0:rows, g:g + 1], sd, MUL, MUL)\
                        .then_inc(S["hp_scaled"], 1)
                if s >= 9:
                    s1 = s - 9
                    dve.wait_ge(S["hp_rot"], s1 + 1)
                    q = QH[R, 2 * s1:2 * s1 + 2, :]
                    sin, cos = (t[R, :].unsqueeze(1).broadcast_to([ROPE, 2, SEQ]) for t in (SINQ, COSQ))
                    V.tensor_tensor(ROT[R, :].rearrange("p (a t) -> p a t", a=2),
                                    PS[R, 4 + s1 % 2, :].rearrange("p (a t) -> p a t", a=2), sin, MUL).then_inc(S["rope_used"], 1)
                    link(V.tensor_tensor(q, q, cos, MUL))
                    V.tensor_tensor(two(q), two(q), ROT[R, :], ADD).then_inc(S["hp_done"], 1)
                    dve.wait_ge(S["hp_done"], s1 + 1)
            for h in range(HEADS1 + 1):
                if h < HEADS1:
                    dve.wait_ge(S["s_ready"], h + 1)
                    if h >= 2:
                        dve.wait_ge(S["pt_ready"], h - 1)
                    v, b = SM1[:, h % 2, :], 4 * (h % 2)
                    ins = V.scalar_tensor_tensor(v, PS[:, h % 2, 0:3 * P], SCALE1, CN[:, C_MASK:C_MASK + 3 * P], MUL, ADD)
                    ins.then_inc(S["s_sb"], 1)
                    dve.wait_ge(S["s_sb"], h + 1)
                    V.reduce_max(SMALL[:, b:b + 1], v[:, 0:P], AX.X, negate=True)
                    V.reduce_max(SMALL[:, b + 1:b + 2], v[:, P:], AX.X, negate=True).then_inc(S["smax_ready"], 1)
                if h >= 1:
                    g = h - 1
                    v, b = SM1[:, g % 2, :], 4 * (g % 2)
                    dve.wait_ge(S["exp_ready"], g + 1)
                    link(V.reciprocal(SMALL[:, b + 2:b + 4], SMALL[:, b + 2:b + 4]))
                    V.tensor_scalar(v[:, 0:P], v[:, 0:P], SMALL[:, b + 2:b + 3], None, MUL)
                    V.tensor_scalar(v[:, P:], v[:, P:], SMALL[:, b + 3:b + 4], None, MUL).then_inc(S["prob_ready"], 1)
            for m in range(KT):
                if m % 2 == 0:
                    dve.wait_ge(S["unit_done"], AT["wo"] + m // 2 + 1)
                V.scalar_tensor_tensor(X[:, m, NMETA:], PS[:, (6 + m) % 8, 0:SEQ], MOD[:, 48 + ADA_GATE1 + m:49 + ADA_GATE1 + m],
                                       X[:, m, NMETA:], MUL, ADD).then_inc(S["res_ready"], 1)
            rstd(3)
            scaled(3, GS[:, 3, :], H, "norm_scaled")
            ffn(1)
            down_used(1, 48 + ADA_GATE2)

            def plain(n, name):
                rstd(n)
                scaled(n, VEC[:, VAT[name]:VAT[name] + KT], H, "h_ready")

            plain(4, "g_ffn1_pre_2")
            ffn(2)
            down_used(2)
            post(5, 0)
            plain(6, "g_mix_pre_2")
            dve.wait_ge(S["f_act"], 1)
            link(V.scalar_tensor_tensor(FROW[0:HEADS2, 4, :], FROW[0:HEADS2, 0, :], 0.0, FROW[0:HEADS2, 3, :], ALU.min, SUB))
            V.tensor_tensor_scan(FROW[0:HEADS2, 5, :], one[0:HEADS2].broadcast_to([HEADS2, TALL]), FROW[0:HEADS2, 4, :],
                                 0.0, MUL, ADD).then_inc(S["f_ready"], 1)
            link(V.memset(CU[:, :, 0:2], 0.0))
            for c in range(2):
                dve.wait_ge(S["c_copied"], 4)
                dve.wait_ge(S["unit_done"], AT["cin"] + 4 + c + 1)
                V.tensor_tensor(CU[:, 2 * c:2 * c + 2, 2:], CC[:, 2 * c:2 * c + 2, :], PS[:, 4 + 2 * c:6 + 2 * c, 0:TALL], MUL)\
                    .then_inc(S["u_ready"], 1)
            dve.wait_ge(S["u_ready"], 2)
            for j in range(3):
                for m in range(4):
                    w = vec("conv_w_2", 4 * j + m)
                    if j == 0:
                        ins = V.tensor_scalar(CC[:, m, :], CU[:, m, 0:TALL], w, None, MUL)
                    else:
                        ins = V.scalar_tensor_tensor(CC[:, m, :], CU[:, m, j:j + TALL], w, CC[:, m, :], MUL, ADD)
                link(ins)
            V.tensor_tensor(CB[:, :, :], CB[:, :, :], CC[:, :, :], MUL).then_inc(S["conv_ready"], 1)
            dve.wait_ge(S["fq_ready"], 1)
            V.tensor_copy(FQ[:, 0:2, :], PS[:, 3, 0:16].rearrange("p (a b) -> p a b", b=HEADS2))
            V.tensor_copy(FQ[0:NMETA, 2, :], PS[0:NMETA, 3, 16:24]).then_inc(S["fq_copied"], 1)
            dve.wait_ge(S["fq_copied"], 1)
            dve.wait_ge(S["fb_copied"], HEADS2)
            for h in range(HEADS2 + 1):
                if h < HEADS2:
                    p, b = h % 2, 16 + 8 * (h % 2)
                    dve.wait_ge(S["s2_ready"], h + 1)
                    if h >= 2:
                        dve.wait_ge(S["pt2_ready"], h - 1)
                    srcs = (PS[:, 2 * p, 0:P], PS[:, 2 * p, P:3 * P], PS[0:NMETA, 2 * p + 1, 0:TALL])
                    for qt, (rows, keys) in enumerate(QT2):
                        ins = V.scalar_tensor_tensor(SM2[0:rows, p, qt, 0:keys], srcs[qt], FQ[0:rows, qt, h:h + 1],
                                                     FB[0:rows, h, 0:keys], ADD, ADD)
                    ins.then_inc(S["s2_sb"], 1)
                    dve.wait_ge(S["s2_sb"], h + 1)
                    for qt, (rows, keys) in enumerate(QT2):
                        diag = SM2[0:rows, p, qt, keys - rows:keys]
                        ins = V.tensor_tensor(diag, diag, CN[0:rows, C_TRI:C_TRI + rows], ADD)
                    link(ins)
                    for qt, (rows, keys) in enumerate(QT2):
                        ins = V.reduce_max(SMALL[0:rows, b + qt:b + qt + 1], SM2[0:rows, p, qt, 0:keys], AX.X, negate=True)
                    ins.then_inc(S["s2_max"], 1)
                if h >= 1:
                    g = h - 1
                    p, b = g % 2, 16 + 8 * (g % 2)
                    dve.wait_ge(S["s2_exp"], g + 1)
                    link(V.reciprocal(SMALL[:, b + 4:b + 7], SMALL[:, b + 4:b + 7]))
                    for qt, (rows, keys) in enumerate(QT2):
                        v = SM2[0:rows, p, qt, 0:keys]
                        ins = V.tensor_scalar(v, v, SMALL[0:rows, b + 4 + qt:b + 5 + qt], None, MUL)
                    ins.then_inc(S["s2_prob"], 1)
            for br, label in enumerate(("attn_br", "conv_br")):
                for m in range(KT):
                    if m % 4 == 0:
                        dve.wait_ge(S["unit_done"], AT[label] + m // 4 + 1)
                        dve.wait_ge(S["gate_ready"], 8)
                    g = GAT[:, br * KT + m, :]
                    ins = V.tensor_tensor(g, g, PS[:, m, 0:TALL], MUL)
                    ins.then_inc(S["mix_part"], 1)
            dve.wait_ge(S["mix_part"], 2 * KT)
            for m in range(KT):
                V.tensor_tensor(H[:, m, :], GAT[:, m, :], GAT[:, KT + m, :], ADD).then_inc(S["mix_ready"], 1)
            for m in range(KT):
                if m % 2 == 0:
                    dve.wait_ge(S["unit_done"], AT["w_out"] + m // 2 + 1)
                V.tensor_copy(YB[:, m, :], PS[:, m % 4, 0:TALL]).then_inc(S["res_ready"], 1)
            post(7, 1)
            plain(8, "g_ffn2_pre_2")
            ffn(3)
            down_used(3)
            post(9, 2)

        @block.tensor
        def _(pe):
            def mm(o, lhsT, rhs, start, stop):
                return nc.tensor.matmul(o, lhsT, rhs, start=start, stop=stop)

            def loaded(u, i=None):
                n = 16 * (u // SLOTS + 1)
                pe.wait_ge(w_loaded[u % SLOTS], n if i is None else i * 16 + n)

            def stat(n):
                T = N_TOK[n]
                for m in range(KT):
                    pe.wait_ge(S["norm_sq"], KT * n + m + 1)
                    ins = mm(PS[:, STAT_BANK[n], 0:T], ones1024, SQ[:, m, 0:T], m == 0, m == KT - 1)
                ins.then_inc(S["norm_stat"], 1)

            def linear(u, banks, src, T, first=None, k0=0):
                loaded(u)
                _, kts, cols = UNITS[u]
                w = slot(u, kts, cols)
                for t, b in enumerate(banks):
                    for k in range(kts):
                        if first is not None and t == 0:
                            pe.wait_ge(S[first[0]], first[1] + k + 1)
                        ins = mm(PS[:, b, 0:T], w[:, k, t * P:(t + 1) * P], src[:, k, 0:T], k == 0, k == kts - 1)
                ins.then_inc(S["unit_done"], 1)

            def ada_rows(s):
                if s >= 1:
                    pe.wait_ge(S["row_copied"], s)
                for h in range(2):
                    u = 2 * s + h
                    loaded(u)
                    w = slot(u, KT, 256)
                    for k in range(KT):
                        g = slice(32 * (k % 4), 32 * (k % 4) + 32)
                        ins = mm(PS[g, 4, h * 256:(h + 1) * 256], CACT[:, k:k + 1].broadcast_to([P, 32]), w[:, k, :], k < 4, k >= 4)
                    ins.then_inc(S["unit_done"], 1)

            def ada_cols(s):
                pe.wait_ge(S["row_copied"], s + 1)
                if s >= 4:
                    pe.wait_ge(S["ada_used"], 1)
                for m in range(4):
                    ins = mm(PS[:, 7, 4 * s + m:4 * s + m + 1], ROWS[:, s % 2, m * P:(m + 1) * P], CN[:, C_SEL:C_SEL + 1], True, True)
                ins.then_inc(S["ada_cols"], 1)

            def ffn(f):
                T, u0, hb = (SEQ if f < 2 else TALL), AT[FFNS[f]], MT * f

                def gate_up(j, q, p, i=None, first=None):
                    if not (isinstance(j, int) and j < 2):
                        pe.wait_ge(S["hid_ready"], j + (hb - 1))
                    for side in range(2):
                        u = u0 + 2 * q + side
                        loaded(u, i)
                        w = slot(u, KT, 256)
                        for t in range(2):
                            for k in range(KT):
                                if first is not None and side == 0 and t == 0:
                                    pe.wait_ge(S["h_ready"], first + k + 1)
                                ins = mm(PS[:, 4 * p + 2 * side + t, 0:T], w[:, k, t * P:(t + 1) * P], H[:, k, 0:T], k == 0, k == KT - 1)
                        ins.then_inc(S["unit_done"], 1)

                gate_up(0, 0, 0, first=KT * FFN_H[f])
                gate_up(1, 1, 1)
                with pe.Fori(1, MT // 2) as i:
                    gate_up(i * 2, 0, 0, i)
                    gate_up(i * 2 + 1, 1, 1, i)
                gate_up(MT - 1, MT - 1, 0)
                u0 += 2 * MT
                pe.wait_ge(S["hid_ready"], hb + MT - 1)
                with pe.Fori(0, 2) as i:
                    for c in range(2):
                        pe.wait_ge(S["res_ready"], i * 4 + (KT * FFN_OUT[f] + 2 * c - 2))
                        for h in range(2):
                            u = u0 + 2 * c + h
                            loaded(u, i)
                            if c == 0 and h == 1:
                                pe.wait_ge(S["hid_ready"], hb + MT)
                            w = slot(u, MT, 256)
                            for t in range(2):
                                for k in range(MT):
                                    ins = mm(PS[:, 4 + 2 * c + t, 0:T], w[:, k, t * P:(t + 1) * P], HID[:, h * MT + k, 0:T],
                                             h == 0 and k == 0, h == 1 and k == MT - 1)
                            ins.then_inc(S["unit_done"], 1)

            pe.wait_ge(S["const_loaded"], 16)
            pe.wait_ge(S["x_loaded"], 16)
            for m in range(KT):
                for a in range(2):
                    c = (m % 2) * SEQ + a * P
                    ins = nc.tensor.transpose(PS[:, m // 2, c:c + P], XIN[:, a, m * P:(m + 1) * P], ident)
                if m % 2:
                    ins.then_inc(S["xt_ready"], 1)
            pe.wait_ge(S["c_loaded"], 16)
            nc.tensor.transpose(PS[:, 5, 0:KT], CROW[:, :], ident[0:KT, 0:KT]).then_inc(S["cact_ready"], 1)
            pe.wait_ge(S["vrow_loaded"], 16 * (len(VROWS) + 4))
            for i in range(2):
                ins = nc.tensor.transpose(PS[:, 7, i * P:(i + 1) * P], VROW[:, i, :], ident)
            ins.then_inc(S["tr_ready"], 1)
            pe.wait_ge(S["meta_loaded"], 16)
            meta = SG[0:NMETA, :, :, :].rearrange("p a b c -> p (a b c)")
            for m in range(KT):
                ins = nc.tensor.transpose(PS[:, 4, m * NMETA:(m + 1) * NMETA], meta[:, m * P:(m + 1) * P], ident[0:NMETA, 0:NMETA])
            ins.then_inc(S["meta_ready"], 1)
            stat(0)
            pe.wait_ge(S["cexp_ready"], 1)
            pe.wait_ge(S["res_ready"], KT)
            pe.wait_ge(S["meta_used"], 1)
            pe.wait_ge(S["tr_used"], 1)
            for s in range(4):
                if s >= 1:
                    ada_cols(s - 1)
                ada_rows(s)
            ada_cols(3)
            pe.wait_ge(S["lrow_dve"], 3)
            pe.wait_ge(S["norm_std"], 1)
            for i, r in enumerate((6, 7, 9, 11, 15, 5)):
                ins = nc.tensor.transpose(PS[:, 6, i * PAIRS:(i + 1) * PAIRS], LROW[0:PAIRS, r, :], ident[0:PAIRS, 0:PAIRS])
            ins.then_inc(S["lam_ready"], 1)
            pe.wait_ge(S["cm_loaded"], 64)
            for i in range(2):
                for k in range(KT):
                    ins = nc.tensor.transpose(PS[:, 2 * i + k // 4, (k % 4) * P:(k % 4 + 1) * P], CRAW[:, i, k, :], ident)
            ins.then_inc(S["ct_ready"], 1)
            for s in range(4, 8):
                ada_rows(s)
                ada_cols(s)
            pe.wait_ge(S["bd_ready"], 4)
            pe.wait_ge(S["ct_used"], 1)
            for i in range(2):
                for k in range(KT):
                    ins = nc.tensor.transpose(PS[:, 2 * i + k // 4, (k % 4) * P:(k % 4 + 1) * P],
                                              BD[:, i, 4 * k:4 * k + 4, :].rearrange("p a b -> p (a b)"), ident)
            ins.then_inc(S["bt_ready"], 1)

            def b_u(kt):
                pe.wait_ge(S["h_ready"], kt + 1)
                if kt == 0:
                    pe.wait_ge(S["bt_used"], 1)
                else:
                    pe.wait_ge(S["prod_ready"], 2 * kt)
                for a in range(2):
                    for q in range(4):
                        rows = slice(32 * q, 32 * q + 32)
                        ins = mm(PS[:, q, a * SEQ:(a + 1) * SEQ], BT[rows, a, kt, :], H[rows, kt, 0:SEQ], True, True)
                ins.then_inc(S["bu_ready"], 1)

            def y_of(kt):
                pe.wait_ge(S["zc_ready"], kt + 1)
                pe.wait_ge(S["zs_ready"], kt + 1)
                if kt >= 2:
                    pe.wait_ge(S["ysum_ready"], kt - 1)
                terms = ((0, ZC, 0), (1, ZS, 1), (2, ZS, 0), (2, ZC, 1))
                for n, (c, z, a) in enumerate(terms):
                    for q in range(4):
                        rows = slice(32 * q, 32 * q + 32)
                        ins = mm(PS[rows, 5 + kt % 2, 0:SEQ], CT[:, c, kt, rows], z[:, q, a, :], n == 0, n == 3)
                ins.then_inc(S["y_ready"], 1)

            b_u(0)
            for s in range(8, 10):
                ada_rows(s)
                ada_cols(s)
            b_u(1)
            for s in range(10, 12):
                ada_rows(s)
                ada_cols(s)
            for kt in range(KT):
                for s in range(12 + 2 * kt, 14 + 2 * kt):
                    ada_rows(s)
                    ada_cols(s)
                if kt + 2 < KT:
                    b_u(kt + 2)
                y_of(kt)
            for c in range(4):
                if c >= 2:
                    pe.wait_ge(S["sig_ready"], 2 * (c - 1))
                linear(AT["glu"] + c, [2 * (c % 2), 2 * (c % 2) + 1], H, SEQ, first=("gelu_ready", 0) if c == 0 else None)
            stat(1)
            ffn(0)
            stat(2)
            u = AT["kva"]
            loaded(u)
            w = slot(u, KT, 288)
            for b, (c0, n) in enumerate(((0, P), (P, P), (192, QK1))):
                for k in range(KT):
                    if b == 0:
                        pe.wait_ge(S["hk_ready"], k + 1)
                    if b == 0 and k == 0:
                        pe.wait_ge(S["norm_std"], 3)
                    ins = mm(PS[0:n, b, 0:SEQ], w[:, k, c0:c0 + n], HK[:, k, :], k == 0, k == KT - 1)
            ins.then_inc(S["unit_done"], 1)
            linear(AT["dq"], [3, 4], H, SEQ, first=("h_ready", KT * 2))
            pe.wait_ge(S["kv_sq"], 5)
            for i, (b, c0) in enumerate(((0, 0), (3, SEQ))):
                for k in range(2):
                    mm(PS[:, 5, c0:c0 + SEQ], ones256, SQ[:, b + k, 0:SEQ], k == 0, k == 1)
            mm(PS[0:QK1, 6, 0:SEQ], blk[0:QK1, 0:QK1], SQ[0:QK1, 2, 0:SEQ], True, True).then_inc(S["kv_stat"], 1)
            pe.wait_ge(S["kv_norm"], 1)
            mm(PS[0:QK1, 7, 0:SEQ], rot[0:QK1, 0:QK1], KR[0:QK1, 0, :], True, True).then_inc(S["kr_rot"], 1)

            def project(s):
                c, i = s // 4, s % 4
                kv = c < 2
                u = AT["kvb"] + c if kv else AT["uq"] + c - 2
                if i == 0:
                    loaded(u)
                cols, per, rows, src = (1024, 128, NOPE, CKV) if kv else (768, QK1, QK1, QA)
                w = slot(u, 2, cols)
                if s >= 2:
                    pe.wait_ge(S["hp_scaled"], s - 1)
                for j in range(2):
                    c0 = (2 * i + j) * per
                    for k in range(2):
                        ins = mm(PS[0:rows, s % 2, j * SEQ:(j + 1) * SEQ], w[:, k, c0:c0 + rows], src[:, k, :], k == 0, k == 1)
                if kv and i == 3:
                    ins.then_inc(S["hp_proj"], 1)
                    heads = w.rearrange("p k (h c) -> p k h c", c=128)
                    if c == 0:
                        pe.wait_ge(S["kr_done"], 1)
                    else:
                        pe.wait_ge(S["v_copied"], 2)
                    for tt in range(2):
                        for k in range(2):
                            ins = mm(PS[:, 6 + tt, :], CKV[:, k, tt * P:(tt + 1) * P], heads[:, k, :, NOPE:], k == 0, k == 1)
                    ins.then_inc(S["unit_done"], 1)
                elif i == 3:
                    ins.then_inc(S["unit_done"], 1)
                else:
                    ins.then_inc(S["hp_proj"], 1)

            def mean_square(s):
                rows = NOPE if s < 8 else QK1
                pe.wait_ge(S["hp_sq"], s + 1)
                if s >= 2:
                    pe.wait_ge(S["hp_std"], s - 1)
                mm(PS[0:rows, 2 + s % 2, :], blk[0:rows, 0:rows], SQH[0:rows, s % 2, :], True, True).then_inc(S["hp_stat"], 1)

            for s in range(18):
                if s < 16:
                    project(s)
                if 1 <= s <= 16:
                    mean_square(s - 1)
                if s >= 10:
                    s1 = s - 10
                    pe.wait_ge(S["hp_scaled"], 8 + s1 + 1)
                    if s1 >= 2:
                        pe.wait_ge(S["rope_used"], s1 - 1)
                    mm(PS[0:QK1, 4 + s1 % 2, :], rot[0:QK1, 0:QK1], QH[0:QK1, 2 * s1:2 * s1 + 2, :].rearrange("p a t -> p (a t)"),
                       True, True).then_inc(S["hp_rot"], 1)
            pe.wait_ge(S["hp_done"], 8)
            pe.wait_ge(S["v_copied"], 4)
            for h in range(HEADS1 + 2):
                if h < HEADS1:
                    if h >= 2:
                        pe.wait_ge(S["s_sb"], h - 1)
                    mm(PS[:, h % 2, 0:P], QH[0:QK1, h, 0:P], KH[0:QK1, h, 0:P], True, True)
                    mm(PS[:, h % 2, P:3 * P], QH[0:QK1, h, P:], KH[0:QK1, h, :], True, True).then_inc(S["s_ready"], 1)
                if 1 <= h <= HEADS1:
                    g = h - 1
                    pe.wait_ge(S["prob_ready"], g + 1)
                    if g >= 2:
                        pe.wait_ge(S["pt_copied"], g - 1)
                    for c in range(3):
                        ins = nc.tensor.transpose(PS[:, 2 + g % 2, c * P:(c + 1) * P], SM1[:, g % 2, c * P:(c + 1) * P], ident)
                    ins.then_inc(S["pt_ready"], 1)
                if h >= 2:
                    g = h - 2
                    pe.wait_ge(S["pt_copied"], g + 1)
                    if g >= 4:
                        pe.wait_ge(S["o_copied"], g // 2 - 1)
                    r = slice(64 * (g % 2), 64 * (g % 2) + 64)
                    o = 4 + g // 2 % 2
                    mm(PS[r, o, 0:SEQ], VT[:, 0, g * VDIM:(g + 1) * VDIM], PT1[:, g % 2, 0:SEQ], True, False)
                    mm(PS[r, o, P:SEQ], VT[:, 1, g * VDIM:(g + 1) * VDIM], PT1[:, g % 2, SEQ:], False, True).then_inc(S["o_ready"], 1)
            for c in range(4):
                linear(AT["wo"] + c, [(6 + 2 * c) % 8, (7 + 2 * c) % 8], OA, SEQ, first=("o_copied", 0) if c == 0 else None)
            stat(3)
            ffn(1)
            stat(4)
            ffn(2)
            stat(5)
            stat(6)
            for i, label in enumerate(("q2", "q2", "k2", "k2")):
                linear(AT[label] + i % 2, [2 * i, 2 * i + 1], H, TALL, first=("h_ready", KT * 5) if i == 0 else None)
            tokens = ((0, P), (P, P), (2 * P, NMETA))
            pe.wait_ge(S["qk_copied"], 2)
            for c in range(2):
                u = AT["v2"] + c
                loaded(u)
                w = slot(u, KT, 256)
                for tt, (t0, n) in enumerate(tokens):
                    for k in range(KT):
                        ins = mm(PS[0:n, tt, c * 256:(c + 1) * 256], H[:, k, t0:t0 + n], w[:, k, :], k == 0, k == KT - 1)
                ins.then_inc(S["unit_done"], 1)
            u = AT["f2"]
            loaded(u)
            w = slot(u, KT, HEADS2)
            for k in range(KT):
                ins = mm(PS[0:HEADS2, 3, 0:TALL], w[:, k, :], H[:, k, :], k == 0, k == KT - 1)
            ins.then_inc(S["unit_done"], 1)
            pe.wait_ge(S["qk_copied"], 4)
            for i in range(6):
                if i >= 2:
                    pe.wait_ge(S["c_copied"], i - 1)
                linear(AT["cin"] + i, [4 + 2 * (i % 2), 5 + 2 * (i % 2)], H, TALL)
            pe.wait_ge(S["v2_copied"], 3)
            pe.wait_ge(S["f_act"], 1)
            for i in range(8):
                if i >= 2:
                    pe.wait_ge(S["gate_ready"], i - 1)
                linear(AT["gates"] + i, [2 * (i % 2), 1 + 2 * (i % 2)], H, TALL)
            pe.wait_ge(S["f_ready"], 1)
            pe.wait_ge(S["gate_ready"], 8)
            for tt, (t0, n) in enumerate(tokens):
                ins = nc.tensor.transpose(PS[0:n, 3, tt * HEADS2:(tt + 1) * HEADS2], FROW[0:HEADS2, 5, t0:t0 + n],
                                          ident[0:HEADS2, 0:HEADS2])
            ins.then_inc(S["fq_ready"], 1)
            pe.wait_ge(S["u_ready"], 2)
            for h in range(HEADS2):
                if h >= 4:
                    pe.wait_ge(S["fb_copied"], h - 3)
                mm(PS[:, 4 + h % 4, 0:TALL], ident[0:HEADS2, h:h + 1].broadcast_to([HEADS2, P]), FROW[0:HEADS2, 5, :], True, True)\
                    .then_inc(S["fb_ready"], 1)
            pe.wait_ge(S["fq_copied"], 1)
            pe.wait_ge(S["fb_copied"], 8)
            for h in range(HEADS2 + 2):
                if h < HEADS2:
                    p, m = h % 2, h // 2
                    r = slice(64 * p, 64 * p + 64)
                    if h >= 2:
                        pe.wait_ge(S["s2_sb"], h - 1)
                    mm(PS[:, 2 * p, 0:P], Q2[r, m, 0:P], K2[r, m, 0:P], True, True)
                    mm(PS[:, 2 * p, P:3 * P], Q2[r, m, P:2 * P], K2[r, m, 0:2 * P], True, True)
                    mm(PS[0:NMETA, 2 * p + 1, 0:TALL], Q2[r, m, 2 * P:], K2[r, m, :], True, True).then_inc(S["s2_ready"], 1)
                if 1 <= h <= HEADS2:
                    g = h - 1
                    p = g % 2
                    pe.wait_ge(S["s2_prob"], g + 1)
                    if g >= 2:
                        pe.wait_ge(S["pt2_copied"], g - 1)
                    for kt, qt, c0 in ((0, 0, 0), (0, 1, 128), (0, 2, 256), (1, 1, 272), (1, 2, 400), (2, 2, 416)):
                        rows, keys = QT2[qt][0], (P, P, NMETA)[kt]
                        ins = nc.tensor.transpose(PS[0:keys, 4 + p, c0:c0 + rows], SM2[0:rows, p, qt, kt * P:kt * P + keys],
                                                  ident[0:rows, 0:rows])
                    ins.then_inc(S["pt2_ready"], 1)
                if h >= 2:
                    g = h - 2
                    p = g % 2
                    pe.wait_ge(S["pt2_copied"], g + 1)
                    if g >= 4:
                        pe.wait_ge(S["o2_copied"], g // 2 - 1)
                    r, o = slice(64 * p, 64 * p + 64), 6 + g // 2 % 2
                    d = slice(g * DH2, (g + 1) * DH2)
                    mm(PS[r, o, 0:TALL], V2[:, 0, d], PT2[:, p, 0:272], True, False)
                    mm(PS[r, o, P:TALL], V2[:, 1, d], PT2[:, p, 272:416], False, False)
                    mm(PS[r, o, 2 * P:TALL], V2[0:NMETA, 2, d], PT2[0:NMETA, p, 416:432], False, True).then_inc(S["o2_ready"], 1)
            for c in range(2):
                if c == 0:
                    pe.wait_ge(S["s2_sb"], HEADS2)
                linear(AT["attn_br"] + c, list(range(4 * c, 4 * c + 4)), O2, TALL, first=("o2_copied", 0) if c == 0 else None)
            pe.wait_ge(S["conv_ready"], 1)
            for c in range(2):
                pe.wait_ge(S["mix_part"], 4 * c + 4)
                linear(AT["conv_br"] + c, list(range(4 * c, 4 * c + 4)), CB, TALL)
            pe.wait_ge(S["mix_part"], 2 * KT)
            for c in range(4):
                if c >= 2:
                    pe.wait_ge(S["res_ready"], KT * R_YM + 2 * (c - 1))
                linear(AT["w_out"] + c, [2 * (c % 2), 2 * (c % 2) + 1], H, TALL, first=("mix_ready", 0) if c == 0 else None)
            stat(7)
            stat(8)
            ffn(3)
            stat(9)
            for b in range(4):
                for m in range(4):
                    f = 4 * (b % 2) + m
                    pe.wait_ge(S["res_ready"], KT * R_X3 + f + 1)
                    t0 = NMETA + (b // 2) * P
                    ins = nc.tensor.transpose(PS[:, b, m * P:(m + 1) * P], X[:, f, t0:t0 + P], ident)
                ins.then_inc(S["out_tr"], 1)


_INS = ["x", "c", "positions", "ada_w", "ada_b", "norm1_g", "norm2_g", "ffn_w_gate", "ffn_w_up", "ffn_w_down",
        "s5_lam_re", "s5_lam_im", "s5_log_dt", "s5_b_re", "s5_b_im", "s5_c_re", "s5_c_im", "s5_d", "s5_w_glu",
        "s5_b_glu", "kv_ada_w", "kv_ada_b", "kv_norm_g", "w_kv_a", "kv_a_norm_g", "w_kv_b", "k_nope_norm_g",
        "k_rope_norm_g", "mla_w_dq", "mla_q_norm_g", "mla_w_uq", "mla_q_nope_norm_g", "mla_q_rope_norm_g",
        "mla_w_o", "meta_tokens_2", "w_in_2", "b_forget_2", "conv_w_2", "w_attn_branch_2", "w_conv_branch_2",
        "w_out_2", "g_ffn1_pre_2", "g_ffn1_post_2", "w_ffn1_in_2", "w_ffn1_out_2", "g_mix_pre_2", "g_mix_post_2",
        "g_ffn2_pre_2", "g_ffn2_post_2", "w_ffn2_in_2", "w_ffn2_out_2"]


def kernel(**inputs):
    import concourse.bacc as _bacc
    from concourse import mybir as _mybir
    from concourse.bass_utils import run_bass_kernel_spmd as _run

    nc = _bacc.Bacc("TRN2", target_bir_lowering=False, num_devices=1)
    arrays, aps = {}, {}

    def give(name, a):
        a = np.ascontiguousarray(a)
        arrays[f"in_{name}"] = a
        aps[name] = nc.dram_tensor(f"in_{name}", a.shape, _mybir.dt.from_np(a.dtype), kind="ExternalInput").ap()

    for name in _INS:
        give(name, inputs[name])
    give("consts", constants())
    out = nc.dram_tensor("out", (1, SEQ, D), _mybir.dt.float32, kind="ExternalOutput").ap()
    build(nc, aps, out)
    return _run(nc, [arrays], core_ids=[0]).results[0]["out"]
```

```python
import math
import numpy as np
import concourse.bass as bass
from concourse import mybir
from contextlib import ExitStack

D = 1024
SEQ = 256
NMETA = 16
TALL = SEQ + NMETA
F = 2816
P = 128
KT = D // P
FT = F // P
EPS = 1e-6
HEADS1, NOPE, ROPE, VDIM = 16, 64, 32, 64
QK1 = NOPE + ROPE
HEADS2, DH2 = 8, 64
GROUPS, GCH, NST = 64, 16, 64
PAIRS = GROUPS // 2
CW = 512
SCALE1 = 1.0 / math.sqrt(QK1)
SCALE2 = DH2 ** -0.5
QT2 = ((128, 128), (128, 256), (16, 272))
NEG = -1e30
MAGIC = 1.5 * 2.0 ** 23
MAGIC14 = 1.5 * 2.0 ** 9
TWO_PI = 2.0 * math.pi
C1 = 6.28125
C2 = float(np.float32(np.round((TWO_PI - C1) * 2 ** 22) / 2 ** 22))
C3 = TWO_PI - C1 - C2
PI_IN = 3.1415925
SLOTS = 4
SLOTF = KT * 288
DOWN_K = (0, 6, 12, 17, 22)

C_ID, C_ONE1024, C_ONE256, C_BLK, C_ROT, C_TRI, C_MASK, C_T = 0, 128, 256, 384, 512, 640, 768, 1152
C_INV, C_EPS, C_HPI, C_ONE, C_SEL, C_END = 1408, 1409, 1410, 1411, 1412, 1413


def constants():
    c = np.zeros((P, C_END), np.float32)
    c[:, C_ID:C_ID + P] = np.eye(P)
    c[:, C_ONE1024:C_ONE1024 + P] = 1.0 / D
    c[:, C_ONE256:C_ONE256 + P] = 1.0 / 256
    c[0:NOPE, C_BLK:C_BLK + NOPE] = 1.0 / NOPE
    c[NOPE:QK1, C_BLK + NOPE:C_BLK + QK1] = 1.0 / ROPE
    for j in range(ROPE // 2):
        c[NOPE + ROPE // 2 + j, C_ROT + NOPE + j] = -1.0
        c[NOPE + j, C_ROT + NOPE + ROPE // 2 + j] = 1.0
    r = np.arange(P)
    c[:, C_TRI:C_TRI + P] = np.where(r[None, :] <= r[:, None], 0.0, NEG)
    half = (r[:, None] < 64) & (r[None, :] >= 64)
    c[:, C_MASK:C_MASK + P] = np.where(half, NEG, 0.0)
    c[:, C_MASK + 2 * P:C_MASK + 3 * P] = np.where(half, NEG, 0.0)
    c[:, C_T:C_T + SEQ] = np.arange(SEQ)
    inv = 1.0 / (np.float32(10000.0) ** (np.arange(0, ROPE, 2, dtype=np.float32) / np.float32(ROPE)))
    c[NOPE:QK1, C_INV] = np.concatenate([inv, inv])
    c[:, C_EPS] = EPS
    c[:, C_HPI] = math.pi / 2
    c[:, C_ONE] = 1.0
    c[0:P:32, C_SEL] = 1.0
    return c


VROWS = [("ada_b", 96), ("kv_ada_b", 16), ("norm1_g", 16), ("norm2_g", 16), ("s5_d", 8), ("s5_b_glu", 8),
         ("kv_norm_g", 8), ("kv_a_norm_g", 2), ("mla_q_norm_g", 2), ("g_ffn1_pre_2", 8), ("g_ffn1_post_2", 8),
         ("g_mix_pre_2", 8), ("g_mix_post_2", 8), ("g_ffn2_pre_2", 8), ("g_ffn2_post_2", 8), ("conv_w_2", 12)]
VAT, _n = {}, 0
for _name, _rows in VROWS:
    VAT[_name] = _n
    _n += _rows
VAT["q96"], VAT["k96"] = _n, _n + 1
assert VAT["norm1_g"] + 16 == P and _n + 2 <= 2 * P


def build(nc, A, out):
    fp32, i32, f32r = mybir.dt.float32, mybir.dt.int32, mybir.dt.float32r
    ALU, ACT, AX = mybir.AluOpType, mybir.ActivationFunctionType, mybir.AxisListType
    MUL, ADD, SUB = ALU.mult, ALU.add, ALU.subtract
    ctx = ExitStack()
    with ctx:
        def sb(name, shape, dt=fp32):
            return ctx.enter_context(nc.sbuf_tensor(name, shape, dt))

        def sem(name):
            return ctx.enter_context(nc.semaphore(name))

        X = sb("X", [P, KT, TALL])
        SQ = sb("SQ", [P, KT, TALL])
        CN = sb("CN", [P, C_END])
        VEC = sb("VEC", [P, 256])
        VROW = sb("VROW", [P, 2, P])
        MOD = sb("MOD", [P, 112])
        GS = sb("GS", [P, 5, KT])
        GH = sb("GH", [P, 3, KT])
        STD = sb("STD", [P, 512])
        RSTD = sb("RSTD", [P, TALL])
        SG = sb("SG", [P, 2, 2, TALL])
        CROW = sb("CROW", [KT, P])
        CACT = sb("CACT", [P, KT])
        SMALL = sb("SMALL", [P, 64])
        BF = sb("BF", [HEADS2, 1])
        with nc.sbuf_tensor("H", [P, KT, TALL], fp32) as H:
            pass
        HH = sb("HH", [P, KT, TALL], f32r)
        with nc.sbuf_tensor("RING", [P, SLOTS, SLOTF], fp32) as RING:
            pass
        WL = sb("WL", [P, SLOTS, SLOTF], f32r)
        with nc.sbuf_tensor("ARENA", [P, 33000], fp32) as ARENA:
            pass
        PARTS = sb("PARTS", [P, 33000], f32r)
        PS = ctx.enter_context(nc.psum_tensor("PS", [P, 8, 512], fp32))

        def arena(at, *shape, area=ARENA):
            n = 1
            for s in shape:
                n *= s
            v = area[:, at:at + n]
            if len(shape) == 2:
                v = v.rearrange("p (a b) -> p a b", b=shape[1])
            if len(shape) == 3:
                v = v.rearrange("p (a b c) -> p a b c", b=shape[1], c=shape[2])
            return v, at + n

        WH, at = arena(0, SLOTS, KT * 256, area=PARTS)
        S5_AT = at
        HL, at = arena(at, KT, TALL, area=PARTS)
        LAYER_AT = at
        TAB, at = arena(S5_AT, 6, 4, SEQ)
        COS, SIN = TAB[:, 0:3, :, :], TAB[:, 3:6, :, :]
        BT, at = arena(at, 2, KT, P)
        CT, at = arena(at, 3, KT, P)
        LAM, at = arena(at, 6, PAIRS)
        ROWS, at = arena(at, 2, 512)
        WORK = at
        PC2, at = arena(at, 8, 2, SEQ)
        PS2, at = arena(at, 8, 2, SEQ)
        ZC, at = arena(at, 4, 2, SEQ)
        ZS, at = arena(at, 4, 2, SEQ)
        assert at <= 33000
        BRAW, at = arena(WORK, 2, PAIRS, GCH)
        BD, at = arena(at, 2, PAIRS, 32)
        CRAW, at = arena(at, 2, KT, P)
        LROW, at = arena(at, 16, P)
        BTMP, at = arena(at, 2, PAIRS, GCH)
        assert at <= 33000
        XIN = SQ[:, :, :].rearrange("p a b -> p (a b)")[:, 0:2 * D].rearrange("p (a b) -> p a b", b=D)
        QH, at = arena(LAYER_AT, HEADS1, SEQ)
        KH, at = arena(at, HEADS1, SEQ)
        VT, at = arena(at, 2, HEADS1 * VDIM)
        HK, at = arena(at, KT, SEQ)
        OAH, _ = arena(at - KT * SEQ, KT, SEQ, area=PARTS)
        OAL, at = arena(at, KT, SEQ, area=PARTS)
        CKV, at = arena(at, 2, SEQ)
        QA, at = arena(at, 2, SEQ)
        KR, at = arena(at, 3, SEQ)
        COSQ, at = arena(at, SEQ)
        SINQ, at = arena(at, SEQ)
        SQH, at = arena(at, 2, 2 * SEQ)
        SDH, at = arena(at, 2, 2 * SEQ)
        ROT, at = arena(at, 2 * SEQ)
        SM1, at = arena(at, 2, 3 * P)
        PT1, at = arena(at, 2, 3 * P)
        POSF, at = arena(at, 2, SEQ)
        assert at <= 33000
        POSI, at = arena(at, SEQ)
        POSI = POSI.bitcast(i32)
        YB, at = arena(LAYER_AT, KT, TALL)
        MIX_AT = at
        HIDH, at = arena(at, FT, TALL, area=PARTS)
        HIDL, at = arena(at, FT, TALL, area=PARTS)
        assert at <= 33000
        HIDHP, HIDLP = (h.rearrange("p (j two) t -> p j two t", two=2) for h in (HIDH, HIDL))
        at = MIX_AT
        Q2, at = arena(at, 4, TALL)
        K2, at = arena(at, 4, TALL)
        V2, at = arena(at, 3, HEADS2 * DH2)
        CB, at = arena(at, 4, TALL)
        CC, at = arena(at, 4, TALL)
        CU, at = arena(at, 4, TALL + 2)
        GAT, at = arena(at, 2 * KT, TALL)
        FROW, at = arena(at, 6, TALL)
        FQ, at = arena(at, 3, HEADS2)
        O2, at = arena(at, 4, TALL)
        FB, at = arena(at, HEADS2, TALL)
        SM2, at = arena(at, 2, 3, TALL)
        PT2, at = arena(at, 2, 432)
        assert at <= 33000, at

        ident = CN[:, C_ID:C_ID + P]
        ones1024 = CN[:, C_ONE1024:C_ONE1024 + P]
        ones256 = CN[:, C_ONE256:C_ONE256 + P]
        blk = CN[:, C_BLK:C_BLK + P]
        rot = CN[:, C_ROT:C_ROT + P]
        eps, hpi, one = CN[:, C_EPS:C_EPS + 1], CN[:, C_HPI:C_HPI + 1], CN[:, C_ONE:C_ONE + 1]

        def vec(name, m):
            return VEC[:, VAT[name] + m:VAT[name] + m + 1]

        def w_view(name, *lead):
            w = A[name]
            for l in lead:
                w = w[l]
            return w.rearrange("(k p) c -> p k c", p=P)

        UNITS = []
        AT = {}

        def stream(label, view, kts, c0, c1, width):
            AT[label] = len(UNITS)
            for c in range(c0, c1, width):
                UNITS.append((view[:, kts[0]:kts[1], c:min(c + width, c1)], kts[1] - kts[0], min(width, c1 - c)))

        def stream_ffn(label, gate, g0, up, u0, down):
            AT[label] = len(UNITS)
            UNITS.extend([("ffn", label, None)] * (FT + 16))
            SPLIT.extend(range(AT[label], len(UNITS)))
            FFN[label] = (gate, g0, up, u0, down)

        FFN = {}
        SPLIT = []
        stream("ada_early", w_view("ada_w", 0), (0, KT), 0, 2 * D, 256)
        stream("ada_late", w_view("ada_w", 0), (0, KT), 2 * D, 6 * D, 256)
        stream("ada1", w_view("ada_w", 1), (0, KT), 0, 6 * D, 256)
        stream("kv_ada", w_view("kv_ada_w"), (0, KT), 0, 2 * D, 256)
        stream("glu", w_view("s5_w_glu", 0), (0, KT), 0, D, 256)
        stream_ffn("ffn0", w_view("ffn_w_gate", 0), 0, w_view("ffn_w_up", 0), 0, w_view("ffn_w_down", 0))
        stream("kva", w_view("w_kv_a"), (0, KT), 0, 288, 288)
        stream("dq", w_view("mla_w_dq", 0), (0, KT), 0, 256, 256)
        stream("kvb", w_view("w_kv_b"), (0, 2), 0, 2048, 1024)
        stream("uq", w_view("mla_w_uq", 0), (0, 2), 0, 1536, 768)
        stream("wo", w_view("mla_w_o", 0), (0, KT), 0, D, 256)
        stream_ffn("ffn1", w_view("ffn_w_gate", 1), 0, w_view("ffn_w_up", 1), 0, w_view("ffn_w_down", 1))
        w1 = w_view("w_ffn1_in_2", 0)
        stream_ffn("ffn2", w1, 0, w1, F // 256, w_view("w_ffn1_out_2", 0))
        wi = w_view("w_in_2", 0)
        stream("q2", wi, (0, KT), 0, 512, 256)
        stream("k2", wi, (0, KT), 512, 1024, 256)
        stream("v2", wi, (0, KT), 1024, 1536, 256)
        stream("f2", wi, (0, KT), 1536, 1544, 8)
        stream("cin", wi, (0, KT), 1544, 3080, 256)
        stream("gates", wi, (0, KT), 3080, 5128, 256)
        stream("attn_br", w_view("w_attn_branch_2", 0), (0, 4), 0, D, 512)
        stream("conv_br", w_view("w_conv_branch_2", 0), (0, 4), 0, D, 512)
        stream("w_out", w_view("w_out_2", 0), (0, KT), 0, D, 256)
        w2 = w_view("w_ffn2_in_2", 0)
        stream_ffn("ffn3", w2, 0, w2, F // 256, w_view("w_ffn2_out_2", 0))

        for _label, _n in (("glu", 4), ("wo", 4), ("q2", 21), ("w_out", 4)):
            SPLIT.extend(range(AT[_label], AT[_label] + _n))
        SPLIT.sort()
        SPLIT_AT = {_u: _n for _n, _u in enumerate(SPLIT)}

        def down_unit(d):
            return (DOWN_K[d % 4 + 1] - DOWN_K[d % 4]) * 256

        def width(u):
            _, a, b = UNITS[u]
            if _ != "ffn":
                return a * b
            d = u - AT[a] - 2 * (FT // 2)
            return KT * 256 if d < 0 else down_unit(d)

        def parts(u, kts, cols):
            return [w[:, u % SLOTS, 0:kts * cols].rearrange("p (k c) -> p k c", c=cols) for w in (WH, WL)]

        def slot(u, kts, cols):
            return RING[:, u % SLOTS, 0:kts * cols].rearrange("p (k c) -> p k c", c=cols)

        w_loaded = [sem(f"w_loaded{s}") for s in range(SLOTS)]
        names = """unit_done rope_used const_loaded x_loaded meta_loaded vrow_zero vrow_loaded c_loaded s5_loaded b_loaded cm_loaded pos_loaded bf_loaded
            tr_ready tr_used lam_ready lam_used bt_ready bt_used ct_ready ct_used bd_ready bd_zero cact_ready cexp_ready lrow_dve lrow_act
            b_terms scan_ready zc_ready zs_ready meta_used row_copied ada_cols turn_sin turn_cos xt_ready res_ready norm_sq norm_stat norm_std norm_scaled h_ready
            ada_used bu_ready bu_used prod_ready v_ready z_ready y_ready ysum_ready gelu_ready sig_ready
            silu_ready hid_ready kv_sq kv_stat kv_std kv_norm kr_rot kr_done hp_proj hp_sq hp_stat hp_std hp_scaled hp_rot hp_done
            v_copied hk_scaled hk_ready s_ready s_sb smax_ready exp_ready prob_ready pt_ready pt_copied o_ready o_copied
            rope_sin rope_ang meta_ready qk_copied v2_copied f_act f_dve f_ready fb_ready fq_ready fb_copied fq_copied
            gelu_hi w_hi w_lo norm_hi hid_hi hid_lo o_hi mix_sum mix_hi s2_ready s2_sb s2_max s2_exp s2_prob pt2_ready pt2_copied o2_ready o2_copied
            c_copied u_ready conv_ready gate_ready ya_ready mix_ready mix_part out_tr out_copied stored
            dve_step act_step pool_step""".split()
        S = {n: sem(n) for n in names}


        R_INIT, R_GLU, R_FFN0, R_WO, R_FFN1, R_Y2, R_X2, R_YM, R_XM, R_Y3, R_X3 = range(11)
        NORM_IN = [R_INIT, R_GLU, R_FFN0, R_WO, R_FFN1, R_Y2, R_X2, R_YM, R_XM, R_Y3]
        STAT_BANK = [6, 4, 0, 6, 0, 0, 0, 4, 4, 0]
        N_TOK = [SEQ] * 4 + [TALL] * 6
        FFNS = ["ffn0", "ffn1", "ffn2", "ffn3"]
        FFN_H = [1, 3, 4, 6]
        FFN_OUT = [R_FFN0, R_FFN1, R_Y2, R_Y3]
        MT = FT // 2
        ADA_SHIFT1, ADA_SCALE1, ADA_GATE1, ADA_SHIFT2, ADA_SCALE2, ADA_GATE2 = range(0, 48, 8)
        KV_SHIFT, KV_SCALE = 96, 104

        SCALED = {0: 0, 1: 1, 2: 2, 3: 3, 4: 4, 6: 5, 8: 6}
        IN_PARTS = {1: 0, 3: 1, 4: 2, 6: 3, 8: 4}

        def x_of(n):
            if n in (5, 7, 9):
                return YB
            return X[:, :, TALL - N_TOK[n]:TALL]

        T_ONE = CN[:, C_T:C_T + SEQ]
        block = ctx.enter_context(nc.Block())

        @block.sync
        def _(sp):
            def take(u, dst, src, iteration=None, per=4):
                if u >= SLOTS:
                    sp.wait_ge(S["unit_done"], u - SLOTS + 1 if iteration is None
                               else iteration * per + (u - SLOTS + 1))
                sp.dma_start(dst, src).then_inc(w_loaded[u % SLOTS], 16)

            u = 0
            while u < len(UNITS):
                view, kts, cols = UNITS[u]
                if view != "ffn":
                    take(u, slot(u, kts, cols), view)
                    u += 1
                    continue
                gate, g0, up, up0, down = FFN[kts]
                gate, up, down = (w.rearrange("p k (n c) -> p k n c", c=256) for w in (gate, up, down))

                def pair(j, q, i):
                    take(u + 2 * q, slot(u + 2 * q, KT, 256), gate[:, :, j + g0, :], i)
                    take(u + 2 * q + 1, slot(u + 2 * q + 1, KT, 256), up[:, :, j + up0, :], i)

                with sp.Fori(0, MT // 2) as i:
                    for q in range(2):
                        pair(i * 2 + q, q, i)
                pair(MT - 1, MT - 1, None)
                u += 2 * MT
                with sp.Fori(0, 2) as i:
                    for d in range(8):
                        k0, k1 = DOWN_K[d % 4], DOWN_K[d % 4 + 1]
                        take(u + d, slot(u + d, k1 - k0, 256), down[:, k0:k1, i * 2 + d // 4, :], i, 8)
                u += 16
            for a in range(2):
                sp.wait_ge(S["out_copied"], 2 * a + 2)
                sp.dma_start(out[0, a * P:(a + 1) * P, :], XIN[:, a, :]).then_inc(S["stored"], 16)
            sp.wait_ge(S["stored"], 32)

        @block.gpsimd
        def _(pool):
            nc.gpsimd.memset(VROW[:, :, :], 0.0).then_inc(S["vrow_zero"], 1)
            nc.gpsimd.memset(BD[:, :, :, :], 0.0).then_inc(S["bd_zero"], 1)
            nc.gpsimd.memset(CT[:, :, :, :], 0.0).then_inc(S["bd_zero"], 1)
            nc.gpsimd.memset(SMALL[:, :], 1.0).then_inc(S["bd_zero"], 1)
            pool.wait_ge(S["vrow_zero"], 1)
            for name, rows in VROWS:
                src = A[name]
                flat = src.rearrange(" ".join("abc"[:len(src.shape)]) + " -> (" + " ".join("abc"[:len(src.shape)]) + ")") \
                    if len(src.shape) > 1 else src
                flat = flat.rearrange("(r c) -> r c", c=P)
                at = VAT[name]
                pool.dma_start(VROW[at % P:at % P + rows, at // P, :], flat).then_inc(S["vrow_loaded"], 16)
            for at, parts in ((VAT["q96"], ("mla_q_nope_norm_g", "mla_q_rope_norm_g")),
                              (VAT["k96"], ("k_nope_norm_g", "k_rope_norm_g"))):
                for name, c0, n in zip(parts, (0, NOPE), (NOPE, ROPE)):
                    src = A[name] if len(A[name].shape) == 2 else A[name].unsqueeze(0)
                    pool.dma_start(VROW[at % P:at % P + 1, 1, c0:c0 + n], src).then_inc(S["vrow_loaded"], 16)
            for i, name in enumerate(("s5_b_re", "s5_b_im")):
                pool.dma_start(BRAW[:, i, :, :], A[name][0].rearrange("(k two) n c -> (two n) k c", two=2))\
                    .then_inc(S["b_loaded"], 16)
            for i, name in enumerate(("s5_c_re", "s5_c_im")):
                for d in range(2):
                    pool.dma_start(CRAW[:, i, :, d * NST:(d + 1) * NST],
                                   A[name][0].rearrange("(k g) c n -> (g c) k n", g=8)).then_inc(S["cm_loaded"], 16)
            f_re, f_im = (LAM[:, k, :].unsqueeze(2).broadcast_to([P, PAIRS, GCH]) for k in (4, 5))
            pool.wait_ge(S["b_loaded"], 32)
            pool.wait_ge(S["bd_zero"], 3)
            pool.wait_ge(S["lam_used"], 1)
            for part, (a, b, op) in enumerate(((0, 1, SUB), (1, 0, ADD))):
                nc.gpsimd.tensor_tensor(BTMP[:, 0, :, :], f_re, BRAW[:, a, :, :], MUL).then_inc(S["b_terms"], 1)
                nc.gpsimd.tensor_tensor(BTMP[:, 1, :, :], f_im, BRAW[:, b, :, :], MUL).then_inc(S["b_terms"], 1)
                pool.wait_ge(S["b_terms"], 2 * part + 2)
                for g in range(2):
                    rows = slice(64 * g, 64 * g + 64)
                    nc.gpsimd.tensor_tensor(BD[rows, part, :, g * GCH:(g + 1) * GCH], BTMP[rows, 0, :, :], BTMP[rows, 1, :, :], op)\
                        .then_inc(S["bd_ready"], 1)
                pool.wait_ge(S["bd_ready"], 2 * part + 2)

            def turned(kt):
                pc, ps = PC2[:, 4 * (kt % 2):4 * (kt % 2) + 4], PS2[:, 4 * (kt % 2):4 * (kt % 2) + 4]
                pool.wait_ge(S["prod_ready"], 2 * kt + 2)
                nc.gpsimd.tensor_tensor(pc[:, :, 0, :], pc[:, :, 0, :], ps[:, :, 1, :], ADD)
                nc.gpsimd.tensor_tensor(pc[:, :, 1, :], pc[:, :, 1, :], ps[:, :, 0, :], SUB).then_inc(S["v_ready"], 1)

            turned(0)
            for kt in range(KT):
                if kt + 1 < KT:
                    turned(kt + 1)
                pool.wait_ge(S["scan_ready"], kt + 1)
                if kt >= 1:
                    pool.wait_ge(S["y_ready"], kt)
                t = SIN[:, kt % 3, :, :].unsqueeze(2).broadcast_to([P, 4, 2, SEQ])
                nc.gpsimd.tensor_tensor(ZS[:, :, :, :], PC2[:, 4 * (kt % 2):4 * (kt % 2) + 4], t, MUL).then_inc(S["zs_ready"], 1)

        @block.scalar
        def _(act):
            steps = [0]

            def link(ins):
                steps[0] += 1
                ins.then_inc(S["act_step"], 1)
                act.wait_ge(S["act_step"], steps[0])

            def squares(n, label=None):
                x, T = x_of(n), N_TOK[n]
                for m in range(KT):
                    if label is not None and m == KT - 2:
                        w_highs(label, 0, 1)
                    act.wait_ge(S["res_ready"], KT * NORM_IN[n] + m + 1)
                    nc.scalar.activation(SQ[:, m, 0:T], x[:, m, :], ACT.Square).then_inc(S["norm_sq"], 1)

            def std(n):
                T = N_TOK[n]
                act.wait_ge(S["norm_stat"], n + 1)
                link(nc.scalar.activation(STD[:, 0:T], PS[:, STAT_BANK[n], 0:T], ACT.Ln, bias=eps))
                nc.scalar.activation(RSTD[:, 0:T], STD[:, 0:T], ACT.Exp, scale=-0.5).then_inc(S["norm_std"], 1)

            def shift(n, col):
                for m in range(KT):
                    act.wait_ge(S["norm_scaled"], KT * SCALED[n] + m + 1)
                    nc.scalar.activation(H[:, m, 0:SEQ], H[:, m, 0:SEQ], ACT.Identity,
                                         bias=MOD[:, col + m:col + m + 1]).then_inc(S["h_ready"], 1)

            def high(n, col=None):
                T = N_TOK[n]
                for m in range(KT):
                    act.wait_ge(S["norm_scaled"], KT * SCALED[n] + m + 1)
                    if col is None:
                        ins = nc.scalar.copy(HH[:, m, 0:T], SQ[:, m, 0:T])
                    else:
                        ins = nc.scalar.activation(HH[:, m, 0:T], SQ[:, m, 0:T], ACT.Identity,
                                                   bias=MOD[:, col + m:col + m + 1])
                    ins.then_inc(S["norm_hi"], 1)

            def w_high(u, i=None, at=None):
                n = 16 * (u // SLOTS + 1)
                act.wait_ge(w_loaded[u % SLOTS], n if i is None else i * 16 + n)
                w = width(u if at is None else at)
                nc.scalar.copy(WH[:, u % SLOTS, 0:w], RING[:, u % SLOTS, 0:w]).then_inc(S["w_hi"], 1)

            def w_highs(label, *which):
                for n in which:
                    w_high(AT[label] + n)

            def silu_ffn(f):
                T, u0, base = (SEQ if f < 2 else TALL), AT[FFNS[f]], MT * f

                def pair(j, p, q, i=None):
                    act.wait_ge(S["unit_done"], j * 2 + (u0 + 2))
                    if not (isinstance(j, int) and j < 2):
                        act.wait_ge(S["hid_lo"], j + (base - 1))
                    nc.scalar.activation(SG[:, p, :, 0:T], PS[:, 4 * p:4 * p + 2, 0:T], ACT.Silu)\
                        .then_inc(S["silu_ready"], 1)
                    w_high(u0 + 2 * q + 4, i)
                    act.wait_ge(S["hid_ready"], j + (base + 1))
                    nc.scalar.copy(HIDHP[:, j, :, 0:T], SG[:, p, :, 0:T]).then_inc(S["hid_hi"], 1)
                    w_high(u0 + 2 * q + 5, i)

                pair(0, 0, 0)
                pair(1, 1, 1)
                with act.Fori(1, 4) as i:
                    pair(i * 2, 0, 0, i)
                    pair(i * 2 + 1, 1, 1, i)
                for j in range(8, MT):
                    pair(j, j % 2, j)
                for d in range(4, 16):
                    w_high(u0 + 2 * MT + d)

            act.dma_start(CN[:, :], A["consts"]).then_inc(S["const_loaded"], 16)
            act.dma_start(XIN[:, :, :], A["x"][0].rearrange("(a p) c -> p a c", p=P)).then_inc(S["x_loaded"], 16)
            act.dma_start(CROW[:, :], A["c"].rearrange("a (k p) -> (a k) p", p=P)).then_inc(S["c_loaded"], 16)
            act.dma_start(LROW[0:PAIRS, 0, :], A["s5_lam_re"][0].rearrange("(k two) n -> k (two n)", two=2)).then_inc(S["s5_loaded"], 16)
            act.dma_start(LROW[0:PAIRS, 1, :], A["s5_lam_im"][0].rearrange("(k two) n -> k (two n)", two=2)).then_inc(S["s5_loaded"], 16)
            act.dma_start(LROW[0:PAIRS, 2, 0:2], A["s5_log_dt"][0].rearrange("(k two) -> k two", two=2)).then_inc(S["s5_loaded"], 16)
            act.dma_start(SG[0:NMETA, :, :, :].rearrange("p a b c -> p (a b c)")[:, 0:D], A["meta_tokens_2"]).then_inc(S["meta_loaded"], 16)
            act.dma_start(BF[:, :], A["b_forget_2"].rearrange("a h -> h a")).then_inc(S["bf_loaded"], 16)
            act.wait_ge(S["cact_ready"], 1)
            nc.scalar.activation(CACT[:, :], PS[:, 5, 0:KT], ACT.Silu).then_inc(S["cexp_ready"], 1)
            squares(0)
            act.wait_ge(S["s5_loaded"], 48)
            nc.scalar.activation(LROW[0:PAIRS, 3, 0:2], LROW[0:PAIRS, 2, 0:2], ACT.Exp).then_inc(S["lrow_act"], 1)
            act.wait_ge(S["lrow_dve"], 1)
            nc.scalar.activation(LROW[0:PAIRS, 6, :], LROW[0:PAIRS, 4, :], ACT.Exp).then_inc(S["lrow_act"], 1)
            act.wait_ge(S["lrow_dve"], 2)
            nc.scalar.activation(LROW[0:PAIRS, 10, :], LROW[0:PAIRS, 8, :], ACT.Sin).then_inc(S["lrow_act"], 1)
            nc.scalar.activation(LROW[0:PAIRS, 11, :], LROW[0:PAIRS, 9, :], ACT.Sin, scale=-1.0, bias=hpi[0:PAIRS])\
                .then_inc(S["lrow_act"], 1)
            std(0)
            def row_copy(s):
                act.wait_ge(S["unit_done"], 2 * s + 2)
                if s >= 2:
                    act.wait_ge(S["ada_cols"], s - 1)
                nc.scalar.copy(ROWS[:, s % 2, :], PS[:, 4, :]).then_inc(S["row_copied"], 1)

            def table(kt):
                act.wait_ge(S["turn_cos"], kt + 1)
                k = kt % 3
                nc.scalar.activation(SIN[:, k, :, :], COS[:, k, :, :], ACT.Sin, scale=2 * PI_IN)
                link(nc.scalar.activation(COS[:, k, :, :], COS[:, k, :, :], ACT.Abs))
                nc.scalar.activation(COS[:, k, :, :], COS[:, k, :, :], ACT.Sin, scale=-TWO_PI, bias=hpi)\
                    .then_inc(S["turn_sin"], 1)

            for s in range(4):
                row_copy(s)
            shift(0, ADA_SHIFT1)
            for s in range(4, 12):
                row_copy(s)
                if s in (7, 9):
                    table((s - 7) // 2)
            for kt in range(KT):
                if kt + 2 < KT:
                    table(kt + 2)
                row_copy(12 + 2 * kt)
                row_copy(13 + 2 * kt)
            w_highs("glu", 0, 1, 2, 3)
            for kt in range(KT):
                act.wait_ge(S["ysum_ready"], kt + 1)
                link(nc.scalar.activation(SQ[:, kt, 0:SEQ], H[:, kt, 0:SEQ], ACT.Gelu_apprx_tanh))
                nc.scalar.copy(HH[:, kt, 0:SEQ], SQ[:, kt, 0:SEQ]).then_inc(S["gelu_hi"], 1)
            for c in range(4):
                act.wait_ge(S["unit_done"], AT["glu"] + c + 1)
                if c >= 2:
                    act.wait_ge(S["res_ready"], KT * R_GLU + 2 * (c - 1))
                for half in range(2):
                    nc.scalar.activation(SG[:, c % 2, half, 0:SEQ], PS[:, 2 * (c % 2) + half, 0:SEQ], ACT.Sigmoid,
                                         bias=vec("s5_b_glu", 2 * c + half)).then_inc(S["sig_ready"], 1)
                if c < 2:
                    w_highs("ffn0", c)
            squares(1)
            std(1)
            high(1, ADA_SHIFT2)
            w_highs("ffn0", 2, 3)
            silu_ffn(0)
            squares(2)
            std(2)
            act.dma_start(POSI[NOPE:QK1, :], A["positions"].broadcast_to([ROPE, SEQ])).then_inc(S["pos_loaded"], 16)
            act.wait_ge(S["rope_ang"], 1)
            nc.scalar.activation(SINQ[NOPE:QK1, :], POSF[NOPE:QK1, 0, :], ACT.Sin)
            nc.scalar.activation(COSQ[NOPE:QK1, :], POSF[NOPE:QK1, 1, :], ACT.Sin, scale=-1.0, bias=hpi[NOPE:QK1])\
                .then_inc(S["rope_sin"], 1)
            for m in range(KT):
                act.wait_ge(S["hk_scaled"], m + 1)
                nc.scalar.activation(HK[:, m, :], HK[:, m, :], ACT.Identity, bias=MOD[:, KV_SHIFT + m:KV_SHIFT + m + 1])\
                    .then_inc(S["hk_ready"], 1)
            shift(2, 48 + ADA_SHIFT1)
            act.wait_ge(S["unit_done"], AT["kva"] + 1)
            for b in range(3):
                rows = P if b < 2 else QK1
                nc.scalar.activation(SQ[0:rows, b, 0:SEQ], PS[0:rows, b, 0:SEQ], ACT.Square).then_inc(S["kv_sq"], 1)
            act.wait_ge(S["unit_done"], AT["dq"] + 1)
            for b in range(3, 5):
                nc.scalar.activation(SQ[:, b, 0:SEQ], PS[:, b, 0:SEQ], ACT.Square).then_inc(S["kv_sq"], 1)
            act.wait_ge(S["kv_stat"], 1)
            nc.scalar.activation(STD[:, :], PS[:, 5, :], ACT.Ln, bias=eps)
            link(nc.scalar.activation(SDH[0:QK1, 0, 0:SEQ], PS[0:QK1, 6, 0:SEQ], ACT.Ln, bias=eps[0:QK1]))
            nc.scalar.activation(STD[:, :], STD[:, :], ACT.Exp, scale=-0.5).then_inc(S["kv_std"], 1)
            nc.scalar.activation(SDH[0:QK1, 0, 0:SEQ], SDH[0:QK1, 0, 0:SEQ], ACT.Exp, scale=-0.5).then_inc(S["kv_std"], 1)
            for s in range(17):
                if s < 16:
                    rows = NOPE if s < 8 else QK1
                    if s in (11, 15):
                        act.wait_ge(S["unit_done"], AT["uq"] + (s - 7) // 4)
                    else:
                        act.wait_ge(S["hp_proj"], s + 1 if s < 11 else s)
                    if s >= 2:
                        act.wait_ge(S["hp_stat"], s - 1)
                    nc.scalar.activation(SQH[0:rows, s % 2, :], PS[0:rows, s % 2, :], ACT.Square).then_inc(S["hp_sq"], 1)
                if s in (4, 8):
                    c = s // 4 - 1
                    act.wait_ge(S["unit_done"], AT["kvb"] + c + 1)
                    for tt in range(2):
                        nc.scalar.copy(VT[:, tt, c * 512:(c + 1) * 512], PS[:, 6 + tt, :]).then_inc(S["v_copied"], 1)
                if s >= 1:
                    s1 = s - 1
                    rows = NOPE if s1 < 8 else QK1
                    act.wait_ge(S["hp_stat"], s1 + 1)
                    if s1 >= 2:
                        act.wait_ge(S["hp_scaled"], s1 - 1)
                    if s1 == 0:
                        act.wait_ge(S["kv_norm"], 1)
                    sd = SDH[0:rows, s1 % 2, :]
                    link(nc.scalar.activation(sd, PS[0:rows, 2 + s1 % 2, :], ACT.Ln, bias=eps[0:rows]))
                    nc.scalar.activation(sd, sd, ACT.Exp, scale=-0.5).then_inc(S["hp_std"], 1)
            for h in range(HEADS1 + 2):
                if h < HEADS1:
                    act.wait_ge(S["smax_ready"], h + 1)
                    q, k = SM1[:, h % 2, 0:P], SM1[:, h % 2, P:3 * P]
                    b = 4 * (h % 2)
                    nc.scalar.activation(q, q, ACT.Exp, bias=SMALL[:, b:b + 1], accum_out=SMALL[:, b + 2:b + 3])
                    nc.scalar.activation(k, k, ACT.Exp, bias=SMALL[:, b + 1:b + 2], accum_out=SMALL[:, b + 3:b + 4])\
                        .then_inc(S["exp_ready"], 1)
                if 1 <= h <= HEADS1:
                    g = h - 1
                    act.wait_ge(S["pt_ready"], g + 1)
                    if g >= 2:
                        act.wait_ge(S["o_ready"], g - 1)
                    nc.scalar.copy(PT1[:, g % 2, :], PS[:, 2 + g % 2, 0:3 * P]).then_inc(S["pt_copied"], 1)
                if h >= 2 and h % 2:
                    g = h - 2
                    act.wait_ge(S["o_ready"], g + 1)
                    nc.scalar.copy(OAH[:, g // 2, :], PS[:, 4 + g // 2 % 2, 0:SEQ]).then_inc(S["o_hi"], 1)
                    if g >= 9:
                        w_highs("wo", (g - 9) // 2)
            w_highs("ffn1", 0, 1)
            squares(3)
            std(3)
            high(3, 48 + ADA_SHIFT2)
            w_highs("ffn1", 2, 3)
            silu_ffn(1)
            squares(4, "ffn2")
            std(4)
            high(4)
            w_highs("ffn2", 2, 3)
            silu_ffn(2)
            squares(5, "q2")
            std(5)
            w_highs("q2", 2, 3)
            squares(6)
            std(6)
            high(6)
            for i, (dst, label) in enumerate(((Q2, "q2"), (Q2, "q2"), (K2, "k2"), (K2, "k2"))):
                c = i % 2
                act.wait_ge(S["unit_done"], AT[label] + c + 1)
                nc.scalar.activation(dst[:, 2 * c:2 * c + 2, :], PS[:, 2 * i:2 * i + 2, 0:TALL], ACT.Copy,
                                     scale=SCALE2 if label == "q2" else 1.0).then_inc(S["qk_copied"], 1)
                w_highs("q2", 4 + i)
            act.wait_ge(S["unit_done"], AT["v2"] + 2)
            for tt, rows in enumerate((P, P, NMETA)):
                nc.scalar.copy(V2[0:rows, tt, :], PS[0:rows, tt, :]).then_inc(S["v2_copied"], 1)
            w_highs("cin", 1, 2)
            act.wait_ge(S["unit_done"], AT["f2"] + 1)
            w_highs("cin", 3)
            act.wait_ge(S["bf_loaded"], 16)
            link(nc.scalar.activation(FROW[0:HEADS2, 0, :], PS[0:HEADS2, 3, 0:TALL], ACT.Identity, bias=BF[:, :]))
            link(nc.scalar.activation(FROW[0:HEADS2, 1, :], FROW[0:HEADS2, 0, :], ACT.Abs))
            link(nc.scalar.activation(FROW[0:HEADS2, 2, :], FROW[0:HEADS2, 1, :], ACT.Exp, scale=-1.0))
            nc.scalar.activation(FROW[0:HEADS2, 3, :], FROW[0:HEADS2, 2, :], ACT.Ln, bias=one[0:HEADS2]).then_inc(S["f_act"], 1)
            for i in range(4):
                dst = CB if i < 2 else CC
                act.wait_ge(S["unit_done"], AT["cin"] + i + 1)
                c = i % 2
                nc.scalar.copy(dst[:, 2 * c:2 * c + 2, :], PS[:, 4 + 2 * c:6 + 2 * c, 0:TALL]).then_inc(S["c_copied"], 1)
                w_highs("cin", 4 + i)
            w_highs("cin", 8, 9)
            for i in range(8):
                act.wait_ge(S["unit_done"], AT["gates"] + i + 1)
                c = i % 2
                nc.scalar.activation(GAT[:, 2 * i:2 * i + 2, :], PS[:, 2 * c:2 * c + 2, 0:TALL], ACT.Sigmoid)\
                    .then_inc(S["gate_ready"], 1)
                if i < 4:
                    w_highs("gates", 4 + i)
            for h in range(HEADS2):
                act.wait_ge(S["fb_ready"], h + 1)
                nc.scalar.activation(FB[:, h, :], PS[:, 4 + h % 4, 0:TALL], ACT.Copy, scale=-1.0).then_inc(S["fb_copied"], 1)
            for h in range(HEADS2 + 2):
                if h < HEADS2:
                    act.wait_ge(S["s2_max"], h + 1)
                    b = 16 + 8 * (h % 2)
                    for qt, (rows, keys) in enumerate(QT2):
                        v = SM2[0:rows, h % 2, qt, 0:keys]
                        ins = nc.scalar.activation(v, v, ACT.Exp, bias=SMALL[0:rows, b + qt:b + qt + 1],
                                                   accum_out=SMALL[0:rows, b + 4 + qt:b + 5 + qt])
                    ins.then_inc(S["s2_exp"], 1)
                if 1 <= h <= HEADS2:
                    g = h - 1
                    act.wait_ge(S["pt2_ready"], g + 1)
                    if g >= 2:
                        act.wait_ge(S["o2_ready"], g - 1)
                    nc.scalar.copy(PT2[:, g % 2, 0:416], PS[:, 4 + g % 2, 0:416])
                    nc.scalar.copy(PT2[0:NMETA, g % 2, 416:432], PS[0:NMETA, 4 + g % 2, 416:432]).then_inc(S["pt2_copied"], 1)
                if h >= 2 and h % 2:
                    g = h - 2
                    act.wait_ge(S["o2_ready"], g + 1)
                    nc.scalar.copy(O2[:, g // 2, :], PS[:, 6 + g // 2 % 2, 0:TALL]).then_inc(S["o2_copied"], 1)
            w_highs("w_out", 0, 1, 2, 3)
            for m in range(KT):
                act.wait_ge(S["mix_sum"], m + 1)
                nc.scalar.copy(HH[:, m, :], SQ[:, m, :]).then_inc(S["mix_hi"], 1)
            squares(7, "ffn3")
            std(7)
            w_highs("ffn3", 2, 3)
            squares(8)
            std(8)
            high(8)
            silu_ffn(3)
            squares(9)
            std(9)
            for b in range(4):
                act.wait_ge(S["out_tr"], b + 1)
                nc.scalar.copy(XIN[:, b // 2, (b % 2) * 512:(b % 2) * 512 + 512], PS[:, b, :]).then_inc(S["out_copied"], 1)

        @block.vector
        def _(dve):
            steps = [0]

            def link(ins):
                steps[0] += 1
                ins.then_inc(S["dve_step"], 1)
                dve.wait_ge(S["dve_step"], steps[0])

            V = nc.vector

            def rstd(n):
                dve.wait_ge(S["norm_std"], n + 1)

            def scaled(n, gains, dst, done):
                x, T = x_of(n), N_TOK[n]
                for m in range(KT):
                    V.scalar_tensor_tensor(dst[:, m, 0:T], x[:, m, :], gains[:, m:m + 1], RSTD[:, 0:T], MUL, MUL)\
                        .then_inc(S[done], 1)

            def low(n, gains, col=None):
                rstd(n)
                x, T = x_of(n), N_TOK[n]
                for m in range(KT + 2):
                    if m < KT:
                        V.scalar_tensor_tensor(SQ[:, m, 0:T], x[:, m, :], gains[:, m:m + 1], RSTD[:, 0:T], MUL, MUL)\
                            .then_inc(S["norm_scaled"], 1)
                    if m >= 2:
                        k = m - 2
                        dve.wait_ge(S["norm_hi"], KT * IN_PARTS[n] + k + 1)
                        if col is None:
                            ins = V.tensor_tensor(HL[:, k, 0:T], SQ[:, k, 0:T], HH[:, k, 0:T].bitcast(fp32), SUB)
                        else:
                            ins = V.scalar_tensor_tensor(HL[:, k, 0:T], SQ[:, k, 0:T], MOD[:, col + k:col + k + 1],
                                                         HH[:, k, 0:T].bitcast(fp32), ADD, SUB)
                        ins.then_inc(S["h_ready"], 1)

            def w_low(u, i=None, at=None):
                n = SPLIT_AT[u] + 1
                dve.wait_ge(S["w_hi"], n if i is None else i * 4 + n)
                w = width(u if at is None else at)
                V.tensor_tensor(WL[:, u % SLOTS, 0:w], RING[:, u % SLOTS, 0:w], WH[:, u % SLOTS, 0:w].bitcast(fp32), SUB)\
                    .then_inc(S["w_lo"], 1)

            def w_lows(label, *which):
                for n in which:
                    w_low(AT[label] + n)

            def ffn(f):
                T, u0, base = (SEQ if f < 2 else TALL), AT[FFNS[f]], MT * f

                def pair(j, p, q, i=None):
                    dve.wait_ge(S["silu_ready"], j + (base + 1))
                    V.tensor_tensor(SG[:, p, :, 0:T], SG[:, p, :, 0:T], PS[:, 4 * p + 2:4 * p + 4, 0:T], MUL)\
                        .then_inc(S["hid_ready"], 1)
                    w_low(u0 + 2 * q + 4, i)
                    dve.wait_ge(S["hid_hi"], j + (base + 1))
                    V.tensor_tensor(HIDLP[:, j, :, 0:T], SG[:, p, :, 0:T], HIDHP[:, j, :, 0:T].bitcast(fp32), SUB)\
                        .then_inc(S["hid_lo"], 1)
                    w_low(u0 + 2 * q + 5, i)

                pair(0, 0, 0)
                pair(1, 1, 1)
                with dve.Fori(1, 4) as i:
                    pair(i * 2, 0, 0, i)
                    pair(i * 2 + 1, 1, 1, i)
                for j in range(8, MT):
                    pair(j, j % 2, j)

            def down_used(f, gate_col=None, following=None):
                u0 = AT[FFNS[f]] + 2 * MT
                for m in range(KT):
                    if m % 2 == 0:
                        c = m // 2
                        if c < 3:
                            for d in range(4 * c + 4, 4 * c + 7):
                                w_low(u0 + d)
                        elif following is not None:
                            w_lows(following, 0, 1)
                        dve.wait_ge(S["unit_done"], u0 + 4 * c + 4)
                    y = PS[:, 4 + m % 4, 0:(SEQ if f < 2 else TALL)]
                    if gate_col is None:
                        V.tensor_copy(YB[:, m, :], y).then_inc(S["res_ready"], 1)
                    else:
                        V.scalar_tensor_tensor(X[:, m, NMETA:], y, MOD[:, gate_col + m:gate_col + m + 1],
                                               X[:, m, NMETA:], MUL, ADD).then_inc(S["res_ready"], 1)
                    if m % 2 and m < KT - 1:
                        w_low(u0 + 4 * (m // 2) + 7)

            def post(n, k, units=None):
                rstd(n)
                for m in range(KT):
                    ins = V.scalar_tensor_tensor(YB[:, m, :], YB[:, m, :], GH[:, k, m:m + 1], RSTD[:, :], MUL, MUL)
                link(ins)
                for m in range(KT):
                    V.tensor_tensor(X[:, m, :], X[:, m, :], YB[:, m, :], ADD).then_inc(S["res_ready"], 1)
                if units is not None:
                    w_lows(*units)

            for b in range(4):
                dve.wait_ge(S["xt_ready"], b + 1)
                V.tensor_copy(X[:, 2 * b:2 * b + 2, NMETA:], PS[:, b, :].rearrange("p (m t) -> p m t", m=2)).then_inc(S["res_ready"], 2)
            dve.wait_ge(S["tr_ready"], 1)
            V.tensor_copy(VEC[:, :], PS[:, 7, 0:256]).then_inc(S["tr_used"], 1)
            dve.wait_ge(S["meta_ready"], 1)
            V.tensor_copy(X[:, :, 0:NMETA], PS[:, 4, 0:KT * NMETA].rearrange("p (m t) -> p m t", m=KT)).then_inc(S["meta_used"], 1)
            L = [LROW[0:PAIRS, r, :] for r in range(16)]
            dt = LROW[0:PAIRS, 3, 0:2].unsqueeze(2).broadcast_to([PAIRS, 2, NST])

            def by_dt(r):
                return LROW[0:PAIRS, r, :].rearrange("p (g n) -> p g n", g=2)

            dve.wait_ge(S["lrow_act"], 1)
            V.tensor_tensor(by_dt(4), by_dt(0), dt, MUL).then_inc(S["lrow_dve"], 1)
            link(V.tensor_tensor(by_dt(5), by_dt(1), dt, MUL))
            link(V.tensor_scalar(L[7], L[5], 1.0 / TWO_PI, MAGIC, MUL, ADD))
            link(V.tensor_scalar(L[7], L[7], MAGIC, None, SUB))
            link(V.scalar_tensor_tensor(L[8], L[7], -C1, L[5], MUL, ADD))
            link(V.scalar_tensor_tensor(L[8], L[7], -C2, L[8], MUL, ADD))
            link(V.scalar_tensor_tensor(L[8], L[7], -C3, L[8], MUL, ADD))
            link(V.tensor_scalar(L[8], L[8], PI_IN, -PI_IN, ALU.min, ALU.max))
            V.scalar_tensor_tensor(L[9], L[8], -1.0, L[8], MUL, ALU.max).then_inc(S["lrow_dve"], 1)
            link(V.tensor_tensor(L[14], L[0], L[0], MUL))
            link(V.tensor_tensor(L[15], L[1], L[1], MUL))
            link(V.tensor_tensor(L[14], L[14], L[15], ADD))
            link(V.reciprocal(L[14], L[14]))
            dve.wait_ge(S["lrow_act"], 4)
            V.tensor_tensor(L[12], L[6], L[11], MUL)
            link(V.tensor_tensor(L[13], L[6], L[10], MUL))
            link(V.tensor_scalar(L[12], L[12], 1.0, None, SUB))
            V.tensor_tensor(L[15], L[12], L[0], MUL)
            link(V.tensor_tensor(L[5], L[13], L[1], MUL))
            link(V.tensor_tensor(L[15], L[15], L[5], ADD))
            link(V.tensor_tensor(L[15], L[15], L[14], MUL))
            V.tensor_tensor(L[5], L[13], L[0], MUL)
            link(V.tensor_tensor(L[4], L[12], L[1], MUL))
            link(V.tensor_tensor(L[5], L[5], L[4], SUB))
            link(V.tensor_tensor(L[5], L[5], L[14], MUL))
            link(V.tensor_scalar(L[7], L[8], 1.0 / TWO_PI, None, MUL))
            link(V.tensor_scalar(L[9], L[7], MAGIC14, MAGIC14, ADD, SUB))
            V.tensor_tensor(L[11], L[7], L[9], SUB).then_inc(S["lrow_dve"], 1)
            def modulation(c0, c1):
                link(V.tensor_tensor(MOD[:, c0:c1], PS[:, 7, c0:c1], VEC[:, c0:c1], ADD))

            def gain(k, col, g):
                return V.scalar_tensor_tensor(GS[:, k, :], MOD[:, col:col + KT], 1.0, VEC[:, g:g + KT], ADD, MUL)

            dve.wait_ge(S["ada_cols"], 4)
            modulation(0, 16)
            gain(0, ADA_SCALE1, VAT["norm1_g"]).then_inc(S["ada_used"], 1)
            dve.wait_ge(S["ada_used"], 1)
            rstd(0)
            scaled(0, GS[:, 0, :], H, "norm_scaled")
            dve.wait_ge(S["bd_zero"], 3)
            dve.wait_ge(S["lam_ready"], 1)
            V.tensor_copy(LAM[:, :, :], PS[:, 6, 0:6 * PAIRS].rearrange("p (a b) -> p a b", b=PAIRS)).then_inc(S["lam_used"], 1)
            dve.wait_ge(S["lam_used"], 1)
            dve.wait_ge(S["ct_ready"], 1)
            for i, (b, sign) in enumerate(((0, 1.0), (0, -1.0), (2, -1.0))):
                for g in range(2):
                    rows = slice(64 * g, 64 * g + 64)
                    src = PS[rows, b:b + 2, :].rearrange("p b (q g c) -> p (b q) g c", g=2, c=GCH)[:, :, g, :]
                    dst = CT[rows, i, :, :].rearrange("p k (q g c) -> p (k q) g c", g=2, c=GCH)[:, :, g, :]
                    ins = V.tensor_scalar(dst, src, sign, None, MUL)
            ins.then_inc(S["ct_used"], 1)

            def turns(kt):
                m, f = SIN[:, kt % 3, :, :], COS[:, kt % 3, :, :]
                lam = [[LAM[:, k, 4 * kt + q:4 * kt + q + 1] for q in range(4)] for k in range(4)]
                for q in range(4):
                    ins = V.tensor_scalar(m[:, q, :], T_ONE, lam[1][q], MAGIC, MUL, ADD)
                link(ins)
                link(V.tensor_scalar(m, m, MAGIC, None, SUB))
                for q in range(4):
                    ins = V.scalar_tensor_tensor(f[:, q, :], T_ONE, lam[2][q], m[:, q, :], MUL, SUB)
                link(ins)
                for q in range(4):
                    ins = V.scalar_tensor_tensor(f[:, q, :], T_ONE, lam[3][q], f[:, q, :], MUL, ADD)
                link(ins)
                V.tensor_scalar(f, f, 0.5, -0.5, ALU.min, ALU.max).then_inc(S["turn_cos"], 1)

            turns(0)
            dve.wait_ge(S["bt_ready"], 1)
            for part in range(2):
                ins = V.tensor_copy(BT[:, part, :, :].rearrange("p k c -> p (k c)"),
                                    PS[:, 2 * part:2 * part + 2, :].rearrange("p b c -> p (b c)"))
            ins.then_inc(S["bt_used"], 1)
            turns(1)

            def turned_in(kt):
                dve.wait_ge(S["turn_sin"], kt + 1)
                dve.wait_ge(S["bu_ready"], kt + 1)
                if kt >= 2:
                    dve.wait_ge(S["zs_ready"], kt - 1)
                bu = PS[:, 0:4, :].rearrange("p q (a t) -> p q a t", a=2)
                for tab, dst in ((COS, PC2), (SIN, PS2)):
                    t = tab[:, kt % 3, :, :].unsqueeze(2).broadcast_to([P, 4, 2, SEQ])
                    V.tensor_tensor(dst[:, 4 * (kt % 2):4 * (kt % 2) + 4], bu, t, MUL).then_inc(S["prod_ready"], 1)

            def y_sum(kt):
                dve.wait_ge(S["y_ready"], kt + 1)
                V.scalar_tensor_tensor(H[:, kt, 0:SEQ], H[:, kt, 0:SEQ], vec("s5_d", kt), PS[:, 5 + kt % 2, 0:SEQ], MUL, ADD)\
                    .then_inc(S["ysum_ready"], 1)

            turned_in(0)
            for kt in range(KT):
                if kt + 1 < KT:
                    turned_in(kt + 1)
                dve.wait_ge(S["v_ready"], kt + 1)
                z = PC2[:, 4 * (kt % 2):4 * (kt % 2) + 4]
                for q in range(4):
                    r = LAM[:, 0, 4 * kt + q:4 * kt + q + 1].broadcast_to([P, SEQ])
                    for a in range(2):
                        ins = V.tensor_tensor_scan(z[:, q, a, :], r, z[:, q, a, :], 0.0, MUL, ADD)
                ins.then_inc(S["scan_ready"], 1)
                dve.wait_ge(S["scan_ready"], kt + 1)
                if kt >= 1:
                    dve.wait_ge(S["y_ready"], kt)
                t = COS[:, kt % 3, :, :].unsqueeze(2).broadcast_to([P, 4, 2, SEQ])
                V.tensor_tensor(ZC[:, :, :, :], z, t, MUL).then_inc(S["zc_ready"], 1)
                if kt + 2 < KT:
                    if kt >= 1:
                        dve.wait_ge(S["zs_ready"], kt)
                    turns(kt + 2)
                if kt >= 1:
                    y_sum(kt - 1)
            w_lows("glu", 0, 1, 2, 3)
            y_sum(KT - 1)
            for kt in range(KT):
                dve.wait_ge(S["gelu_hi"], kt + 1)
                V.tensor_tensor(HL[:, kt, 0:SEQ], SQ[:, kt, 0:SEQ], HH[:, kt, 0:SEQ].bitcast(fp32), SUB).then_inc(S["gelu_ready"], 1)
            dve.wait_ge(S["ada_cols"], 28)
            modulation(16, 112)
            gain(1, ADA_SCALE2, VAT["norm2_g"])
            gain(2, 48 + ADA_SCALE1, VAT["norm1_g"] + KT)
            gain(3, 48 + ADA_SCALE2, VAT["norm2_g"] + KT)
            gain(4, KV_SCALE, VAT["kv_norm_g"])
            for k, (name, c) in enumerate((("g_ffn1_post_2", 0.5), ("g_mix_post_2", 1.0), ("g_ffn2_post_2", 0.5))):
                ins = V.tensor_scalar(GH[:, k, :], VEC[:, VAT[name]:VAT[name] + KT], c, None, MUL)
            link(ins)
            for m in range(KT):
                dve.wait_ge(S["sig_ready"], m + 1)
                v = SG[:, m // 2 % 2, m % 2, 0:SEQ]
                link(V.tensor_tensor(v, v, SQ[:, m, 0:SEQ], MUL))
                V.scalar_tensor_tensor(X[:, m, NMETA:], v, MOD[:, ADA_GATE1 + m:ADA_GATE1 + m + 1], X[:, m, NMETA:], MUL, ADD)\
                    .then_inc(S["res_ready"], 1)
                if m in (1, 3):
                    w_lows("ffn0", m // 2)
            low(1, GS[:, 1, :], ADA_SHIFT2)
            w_lows("ffn0", 2, 3)
            ffn(0)
            down_used(0, ADA_GATE2)
            dve.wait_ge(S["pos_loaded"], 16)
            R = slice(NOPE, QK1)
            link(V.tensor_copy(POSF[R, 0, :], POSI[R, :]))
            link(V.tensor_scalar(POSF[R, 0, :], POSF[R, 0, :], CN[R, C_INV:C_INV + 1], None, MUL))
            link(V.tensor_scalar(POSF[R, 1, :], POSF[R, 0, :], 1.0 / TWO_PI, MAGIC, MUL, ADD))
            link(V.tensor_scalar(POSF[R, 1, :], POSF[R, 1, :], MAGIC, None, SUB))
            for c in (C1, C2, C3):
                link(V.scalar_tensor_tensor(POSF[R, 0, :], POSF[R, 1, :], -c, POSF[R, 0, :], MUL, ADD))
            link(V.tensor_scalar(POSF[R, 0, :], POSF[R, 0, :], PI_IN, -PI_IN, ALU.min, ALU.max))
            V.scalar_tensor_tensor(POSF[R, 1, :], POSF[R, 0, :], -1.0, POSF[R, 0, :], MUL, ALU.max).then_inc(S["rope_ang"], 1)
            rstd(2)
            scaled(2, GS[:, 4, :], HK, "hk_scaled")
            scaled(2, GS[:, 2, :], H, "norm_scaled")
            dve.wait_ge(S["kv_std"], 2)
            for i in range(2):
                V.scalar_tensor_tensor(CKV[:, i, :], PS[:, i, 0:SEQ], vec("kv_a_norm_g", i), STD[:, 0:SEQ], MUL, MUL)
                V.scalar_tensor_tensor(QA[:, i, :], PS[:, 3 + i, 0:SEQ], vec("mla_q_norm_g", i), STD[:, SEQ:], MUL, MUL)
            V.scalar_tensor_tensor(KR[0:QK1, 0, :], PS[0:QK1, 2, 0:SEQ], VEC[0:QK1, VAT["k96"]:VAT["k96"] + 1],
                                   SDH[0:QK1, 0, 0:SEQ], MUL, MUL).then_inc(S["kv_norm"], 1)
            dve.wait_ge(S["rope_sin"], 1)
            dve.wait_ge(S["kr_rot"], 1)
            V.tensor_tensor(KR[R, 1, :], PS[R, 7, 0:SEQ], SINQ[R, :], MUL)
            link(V.tensor_tensor(KR[R, 2, :], KR[R, 0, :], COSQ[R, :], MUL))
            link(V.tensor_tensor(KR[R, 1, :], KR[R, 1, :], KR[R, 2, :], ADD))
            V.tensor_copy(KH[R, :, :], KR[R, 1, :].unsqueeze(1).broadcast_to([ROPE, HEADS1, SEQ])).then_inc(S["kr_done"], 1)

            def two(ap):
                return ap.rearrange("p a t -> p (a t)")

            for s in range(17):
                if s < 16:
                    rows, dst, g = (NOPE, KH, VAT["k96"]) if s < 8 else (QK1, QH, VAT["q96"])
                    h = 2 * (s % 8)
                    dve.wait_ge(S["hp_std"], s + 1)
                    sd = SDH[0:rows, s % 2, :]
                    V.scalar_tensor_tensor(two(dst[0:rows, h:h + 2, :]), PS[0:rows, s % 2, :], VEC[0:rows, g:g + 1], sd, MUL, MUL)\
                        .then_inc(S["hp_scaled"], 1)
                if s >= 9:
                    s1 = s - 9
                    dve.wait_ge(S["hp_rot"], s1 + 1)
                    q = QH[R, 2 * s1:2 * s1 + 2, :]
                    sin, cos = (t[R, :].unsqueeze(1).broadcast_to([ROPE, 2, SEQ]) for t in (SINQ, COSQ))
                    V.tensor_tensor(ROT[R, :].rearrange("p (a t) -> p a t", a=2),
                                    PS[R, 4 + s1 % 2, :].rearrange("p (a t) -> p a t", a=2), sin, MUL).then_inc(S["rope_used"], 1)
                    link(V.tensor_tensor(q, q, cos, MUL))
                    V.tensor_tensor(two(q), two(q), ROT[R, :], ADD).then_inc(S["hp_done"], 1)
                    dve.wait_ge(S["hp_done"], s1 + 1)
            def heads_low(k):
                dve.wait_ge(S["o_hi"], k + 1)
                V.tensor_tensor(OAL[:, k, :], PS[:, 4 + k % 2, 0:SEQ], OAH[:, k, :].bitcast(fp32), SUB).then_inc(S["o_copied"], 1)

            for h in range(HEADS1 + 1):
                if h < HEADS1:
                    dve.wait_ge(S["s_ready"], h + 1)
                    if h >= 2:
                        dve.wait_ge(S["pt_ready"], h - 1)
                    v, b = SM1[:, h % 2, :], 4 * (h % 2)
                    ins = V.scalar_tensor_tensor(v, PS[:, h % 2, 0:3 * P], SCALE1, CN[:, C_MASK:C_MASK + 3 * P], MUL, ADD)
                    ins.then_inc(S["s_sb"], 1)
                    dve.wait_ge(S["s_sb"], h + 1)
                    V.reduce_max(SMALL[:, b:b + 1], v[:, 0:P], AX.X, negate=True)
                    V.reduce_max(SMALL[:, b + 1:b + 2], v[:, P:], AX.X, negate=True).then_inc(S["smax_ready"], 1)
                if h >= 1:
                    g = h - 1
                    v, b = SM1[:, g % 2, :], 4 * (g % 2)
                    dve.wait_ge(S["exp_ready"], g + 1)
                    link(V.reciprocal(SMALL[:, b + 2:b + 4], SMALL[:, b + 2:b + 4]))
                    V.tensor_scalar(v[:, 0:P], v[:, 0:P], SMALL[:, b + 2:b + 3], None, MUL)
                    V.tensor_scalar(v[:, P:], v[:, P:], SMALL[:, b + 3:b + 4], None, MUL).then_inc(S["prob_ready"], 1)
                if h >= 5 and h % 2:
                    heads_low((h - 5) // 2)
            for k in (6, 7):
                heads_low(k)
            w_lows("wo", 0, 1, 2, 3)
            for m in range(KT):
                if m % 2 == 0:
                    dve.wait_ge(S["unit_done"], AT["wo"] + m // 2 + 1)
                V.scalar_tensor_tensor(X[:, m, NMETA:], PS[:, (6 + m) % 8, 0:SEQ], MOD[:, 48 + ADA_GATE1 + m:49 + ADA_GATE1 + m],
                                       X[:, m, NMETA:], MUL, ADD).then_inc(S["res_ready"], 1)
                if m == 1:
                    w_lows("ffn1", 0, 1)
            low(3, GS[:, 3, :], 48 + ADA_SHIFT2)
            w_lows("ffn1", 2, 3)
            ffn(1)
            down_used(1, 48 + ADA_GATE2, "ffn2")

            def gains(name):
                return VEC[:, VAT[name]:VAT[name] + KT]

            low(4, gains("g_ffn1_pre_2"))
            w_lows("ffn2", 2, 3)
            ffn(2)
            down_used(2, None, "q2")
            post(5, 0, ("q2", 2, 3))
            low(6, gains("g_mix_pre_2"))
            w_lows("q2", *range(4, 11))
            dve.wait_ge(S["f_act"], 1)
            link(V.scalar_tensor_tensor(FROW[0:HEADS2, 4, :], FROW[0:HEADS2, 0, :], 0.0, FROW[0:HEADS2, 3, :], ALU.min, SUB))
            V.tensor_tensor_scan(FROW[0:HEADS2, 5, :], one[0:HEADS2].broadcast_to([HEADS2, TALL]), FROW[0:HEADS2, 4, :],
                                 0.0, MUL, ADD).then_inc(S["f_ready"], 1)
            link(V.memset(CU[:, :, 0:2], 0.0))
            w_lows("cin", 4, 5, 6, 7)
            for c in range(2):
                dve.wait_ge(S["c_copied"], 4)
                dve.wait_ge(S["unit_done"], AT["cin"] + 4 + c + 1)
                V.tensor_tensor(CU[:, 2 * c:2 * c + 2, 2:], CC[:, 2 * c:2 * c + 2, :], PS[:, 4 + 2 * c:6 + 2 * c, 0:TALL], MUL)\
                    .then_inc(S["u_ready"], 1)
                w_lows("cin", 8 + c)
            dve.wait_ge(S["u_ready"], 2)
            for j in range(3):
                for m in range(4):
                    w = vec("conv_w_2", 4 * j + m)
                    if j == 0:
                        ins = V.tensor_scalar(CC[:, m, :], CU[:, m, 0:TALL], w, None, MUL)
                    else:
                        ins = V.scalar_tensor_tensor(CC[:, m, :], CU[:, m, j:j + TALL], w, CC[:, m, :], MUL, ADD)
                link(ins)
                w_lows("gates", 4 + j)
            V.tensor_tensor(CB[:, :, :], CB[:, :, :], CC[:, :, :], MUL).then_inc(S["conv_ready"], 1)
            w_lows("gates", 7)
            dve.wait_ge(S["fq_ready"], 1)
            V.tensor_copy(FQ[:, 0:2, :], PS[:, 3, 0:16].rearrange("p (a b) -> p a b", b=HEADS2))
            V.tensor_copy(FQ[0:NMETA, 2, :], PS[0:NMETA, 3, 16:24]).then_inc(S["fq_copied"], 1)
            dve.wait_ge(S["fq_copied"], 1)
            dve.wait_ge(S["fb_copied"], HEADS2)
            for h in range(HEADS2 + 1):
                if h < HEADS2:
                    p, b = h % 2, 16 + 8 * (h % 2)
                    dve.wait_ge(S["s2_ready"], h + 1)
                    if h >= 2:
                        dve.wait_ge(S["pt2_ready"], h - 1)
                    srcs = (PS[:, 2 * p, 0:P], PS[:, 2 * p, P:3 * P], PS[0:NMETA, 2 * p + 1, 0:TALL])
                    for qt, (rows, keys) in enumerate(QT2):
                        ins = V.scalar_tensor_tensor(SM2[0:rows, p, qt, 0:keys], srcs[qt], FQ[0:rows, qt, h:h + 1],
                                                     FB[0:rows, h, 0:keys], ADD, ADD)
                    ins.then_inc(S["s2_sb"], 1)
                    dve.wait_ge(S["s2_sb"], h + 1)
                    for qt, (rows, keys) in enumerate(QT2):
                        diag = SM2[0:rows, p, qt, keys - rows:keys]
                        ins = V.tensor_tensor(diag, diag, CN[0:rows, C_TRI:C_TRI + rows], ADD)
                    link(ins)
                    for qt, (rows, keys) in enumerate(QT2):
                        ins = V.reduce_max(SMALL[0:rows, b + qt:b + qt + 1], SM2[0:rows, p, qt, 0:keys], AX.X, negate=True)
                    ins.then_inc(S["s2_max"], 1)
                if h >= 1:
                    g = h - 1
                    p, b = g % 2, 16 + 8 * (g % 2)
                    dve.wait_ge(S["s2_exp"], g + 1)
                    link(V.reciprocal(SMALL[:, b + 4:b + 7], SMALL[:, b + 4:b + 7]))
                    for qt, (rows, keys) in enumerate(QT2):
                        v = SM2[0:rows, p, qt, 0:keys]
                        ins = V.tensor_scalar(v, v, SMALL[0:rows, b + 4 + qt:b + 5 + qt], None, MUL)
                    ins.then_inc(S["s2_prob"], 1)
            for br, label in enumerate(("attn_br", "conv_br")):
                for m in range(KT):
                    if m % 4 == 0:
                        dve.wait_ge(S["unit_done"], AT[label] + m // 4 + 1)
                        dve.wait_ge(S["gate_ready"], 8)
                    g = GAT[:, br * KT + m, :]
                    ins = V.tensor_tensor(g, g, PS[:, m, 0:TALL], MUL)
                    ins.then_inc(S["mix_part"], 1)
            w_lows("w_out", 0, 1, 2, 3)
            dve.wait_ge(S["mix_part"], 2 * KT)
            for m in range(KT + 2):
                if m < KT:
                    V.tensor_tensor(SQ[:, m, :], GAT[:, m, :], GAT[:, KT + m, :], ADD).then_inc(S["mix_sum"], 1)
                if m >= 2:
                    dve.wait_ge(S["mix_hi"], m - 1)
                    V.tensor_tensor(HL[:, m - 2, :], SQ[:, m - 2, :], HH[:, m - 2, :].bitcast(fp32), SUB).then_inc(S["mix_ready"], 1)
            for m in range(KT):
                if m % 2 == 0:
                    dve.wait_ge(S["unit_done"], AT["w_out"] + m // 2 + 1)
                V.tensor_copy(YB[:, m, :], PS[:, m % 4, 0:TALL]).then_inc(S["res_ready"], 1)
                if m == 5:
                    w_lows("ffn3", 0, 1)
            post(7, 1, ("ffn3", 2, 3))
            low(8, gains("g_ffn2_pre_2"))
            ffn(3)
            down_used(3)
            post(9, 2)

        @block.tensor
        def _(pe):
            def mm(o, lhsT, rhs, start, stop):
                return nc.tensor.matmul(o, lhsT, rhs, start=start, stop=stop)

            def loaded(u, i=None):
                n = 16 * (u // SLOTS + 1)
                pe.wait_ge(w_loaded[u % SLOTS], n if i is None else i * 16 + n)

            def stat(n):
                T = N_TOK[n]
                for m in range(KT):
                    pe.wait_ge(S["norm_sq"], KT * n + m + 1)
                    ins = mm(PS[:, STAT_BANK[n], 0:T], ones1024, SQ[:, m, 0:T], m == 0, m == KT - 1)
                ins.then_inc(S["norm_stat"], 1)

            def linear(u, banks, src, T, first=None, k0=0):
                loaded(u)
                _, kts, cols = UNITS[u]
                w = slot(u, kts, cols)
                for t, b in enumerate(banks):
                    for k in range(kts):
                        if first is not None and t == 0:
                            pe.wait_ge(S[first[0]], first[1] + k + 1)
                        ins = mm(PS[:, b, 0:T], w[:, k, t * P:(t + 1) * P], src[:, k, 0:T], k == 0, k == kts - 1)
                ins.then_inc(S["unit_done"], 1)

            def split(u, i=None, per=4):
                n = SPLIT_AT[u] + 1
                pe.wait_ge(S["w_lo"], n if i is None else i * per + n)

            def mm3(o, w, x, start, stop):
                (wh, wl), (xh, xl) = w, x
                mm(o, wl, xh, start, False)
                mm(o, wh, xh, False, False)
                return mm(o, wh, xl, False, stop)

            def linear3(u, banks, src, T, first=None):
                split(u)
                _, kts, cols = UNITS[u]
                w = parts(u, kts, cols)
                for t, b in enumerate(banks):
                    for k in range(kts):
                        if first is not None and t == 0:
                            pe.wait_ge(S[first[0]], first[1] + k + 1)
                        ins = mm3(PS[:, b, 0:T], [v[:, k, t * P:(t + 1) * P] for v in w], [v[:, k, 0:T] for v in src],
                                  k == 0, k == kts - 1)
                ins.then_inc(S["unit_done"], 1)

            def ada_rows(s):
                if s >= 1:
                    pe.wait_ge(S["row_copied"], s)
                for h in range(2):
                    u = 2 * s + h
                    loaded(u)
                    w = slot(u, KT, 256)
                    for k in range(KT):
                        g = slice(32 * (k % 4), 32 * (k % 4) + 32)
                        ins = mm(PS[g, 4, h * 256:(h + 1) * 256], CACT[:, k:k + 1].broadcast_to([P, 32]), w[:, k, :], k < 4, k >= 4)
                    ins.then_inc(S["unit_done"], 1)

            def ada_cols(s):
                pe.wait_ge(S["row_copied"], s + 1)
                if s >= 4:
                    pe.wait_ge(S["ada_used"], 1)
                for m in range(4):
                    ins = mm(PS[:, 7, 4 * s + m:4 * s + m + 1], ROWS[:, s % 2, m * P:(m + 1) * P], CN[:, C_SEL:C_SEL + 1], True, True)
                ins.then_inc(S["ada_cols"], 1)

            def ffn(f):
                T, u0, hb = (SEQ if f < 2 else TALL), AT[FFNS[f]], MT * f

                def gate_up(j, q, p, i=None, first=None):
                    if not (isinstance(j, int) and j < 2):
                        pe.wait_ge(S["hid_ready"], j + (hb - 1))
                    for side in range(2):
                        u = u0 + 2 * q + side
                        split(u, i)
                        w = parts(u, KT, 256)
                        for t in range(2):
                            for k in range(KT):
                                if first is not None and side == 0 and t == 0:
                                    pe.wait_ge(S["h_ready"], first + k + 1)
                                ins = mm3(PS[:, 4 * p + 2 * side + t, 0:T], [v[:, k, t * P:(t + 1) * P] for v in w],
                                          [v[:, k, 0:T] for v in (HH, HL)], k == 0, k == KT - 1)
                        ins.then_inc(S["unit_done"], 1)

                gate_up(0, 0, 0, first=KT * FFN_H[f])
                gate_up(1, 1, 1)
                with pe.Fori(1, MT // 2) as i:
                    gate_up(i * 2, 0, 0, i)
                    gate_up(i * 2 + 1, 1, 1, i)
                gate_up(MT - 1, MT - 1, 0)
                u0 += 2 * MT
                pe.wait_ge(S["hid_ready"], hb + MT - 1)
                pe.wait_ge(S["hid_lo"], hb + MT - 1)
                with pe.Fori(0, 2) as i:
                    for c in range(2):
                        pe.wait_ge(S["res_ready"], i * 4 + (KT * FFN_OUT[f] + 2 * c - 2))
                        for h in range(4):
                            u, k0, k1 = u0 + 4 * c + h, DOWN_K[h], DOWN_K[h + 1]
                            split(u, i, 8)
                            if c == 0 and h == 3:
                                pe.wait_ge(S["hid_lo"], hb + MT)
                            w = parts(u, k1 - k0, 256)
                            for t in range(2):
                                for k in range(k0, k1):
                                    ins = mm3(PS[:, 4 + 2 * c + t, 0:T], [v[:, k - k0, t * P:(t + 1) * P] for v in w],
                                              [v[:, k, 0:T] for v in (HIDH, HIDL)], k == 0, k == FT - 1)
                            ins.then_inc(S["unit_done"], 1)

            pe.wait_ge(S["const_loaded"], 16)
            pe.wait_ge(S["x_loaded"], 16)
            for m in range(KT):
                for a in range(2):
                    c = (m % 2) * SEQ + a * P
                    ins = nc.tensor.transpose(PS[:, m // 2, c:c + P], XIN[:, a, m * P:(m + 1) * P], ident)
                if m % 2:
                    ins.then_inc(S["xt_ready"], 1)
            pe.wait_ge(S["c_loaded"], 16)
            nc.tensor.transpose(PS[:, 5, 0:KT], CROW[:, :], ident[0:KT, 0:KT]).then_inc(S["cact_ready"], 1)
            pe.wait_ge(S["vrow_loaded"], 16 * (len(VROWS) + 4))
            for i in range(2):
                ins = nc.tensor.transpose(PS[:, 7, i * P:(i + 1) * P], VROW[:, i, :], ident)
            ins.then_inc(S["tr_ready"], 1)
            pe.wait_ge(S["meta_loaded"], 16)
            meta = SG[0:NMETA, :, :, :].rearrange("p a b c -> p (a b c)")
            for m in range(KT):
                ins = nc.tensor.transpose(PS[:, 4, m * NMETA:(m + 1) * NMETA], meta[:, m * P:(m + 1) * P], ident[0:NMETA, 0:NMETA])
            ins.then_inc(S["meta_ready"], 1)
            stat(0)
            pe.wait_ge(S["cexp_ready"], 1)
            pe.wait_ge(S["res_ready"], KT)
            pe.wait_ge(S["meta_used"], 1)
            pe.wait_ge(S["tr_used"], 1)
            for s in range(4):
                if s >= 1:
                    ada_cols(s - 1)
                ada_rows(s)
            ada_cols(3)
            pe.wait_ge(S["lrow_dve"], 3)
            pe.wait_ge(S["norm_std"], 1)
            for i, r in enumerate((6, 7, 9, 11, 15, 5)):
                ins = nc.tensor.transpose(PS[:, 6, i * PAIRS:(i + 1) * PAIRS], LROW[0:PAIRS, r, :], ident[0:PAIRS, 0:PAIRS])
            ins.then_inc(S["lam_ready"], 1)
            pe.wait_ge(S["cm_loaded"], 64)
            for i in range(2):
                for k in range(KT):
                    ins = nc.tensor.transpose(PS[:, 2 * i + k // 4, (k % 4) * P:(k % 4 + 1) * P], CRAW[:, i, k, :], ident)
            ins.then_inc(S["ct_ready"], 1)
            for s in range(4, 8):
                ada_rows(s)
                ada_cols(s)
            pe.wait_ge(S["bd_ready"], 4)
            pe.wait_ge(S["ct_used"], 1)
            for i in range(2):
                for k in range(KT):
                    ins = nc.tensor.transpose(PS[:, 2 * i + k // 4, (k % 4) * P:(k % 4 + 1) * P],
                                              BD[:, i, 4 * k:4 * k + 4, :].rearrange("p a b -> p (a b)"), ident)
            ins.then_inc(S["bt_ready"], 1)

            def b_u(kt):
                pe.wait_ge(S["h_ready"], kt + 1)
                if kt == 0:
                    pe.wait_ge(S["bt_used"], 1)
                else:
                    pe.wait_ge(S["prod_ready"], 2 * kt)
                for a in range(2):
                    for q in range(4):
                        rows = slice(32 * q, 32 * q + 32)
                        ins = mm(PS[:, q, a * SEQ:(a + 1) * SEQ], BT[rows, a, kt, :], H[rows, kt, 0:SEQ], True, True)
                ins.then_inc(S["bu_ready"], 1)

            def y_of(kt):
                pe.wait_ge(S["zc_ready"], kt + 1)
                pe.wait_ge(S["zs_ready"], kt + 1)
                if kt >= 2:
                    pe.wait_ge(S["ysum_ready"], kt - 1)
                terms = ((0, ZC, 0), (1, ZS, 1), (2, ZS, 0), (2, ZC, 1))
                for n, (c, z, a) in enumerate(terms):
                    for q in range(4):
                        rows = slice(32 * q, 32 * q + 32)
                        ins = mm(PS[rows, 5 + kt % 2, 0:SEQ], CT[:, c, kt, rows], z[:, q, a, :], n == 0, n == 3)
                ins.then_inc(S["y_ready"], 1)

            b_u(0)
            for s in range(8, 10):
                ada_rows(s)
                ada_cols(s)
            b_u(1)
            for s in range(10, 12):
                ada_rows(s)
                ada_cols(s)
            for kt in range(KT):
                for s in range(12 + 2 * kt, 14 + 2 * kt):
                    ada_rows(s)
                    ada_cols(s)
                if kt + 2 < KT:
                    b_u(kt + 2)
                y_of(kt)
            for c in range(4):
                if c >= 2:
                    pe.wait_ge(S["sig_ready"], 2 * (c - 1))
                linear3(AT["glu"] + c, [2 * (c % 2), 2 * (c % 2) + 1], (HH, HL), SEQ, first=("gelu_ready", 0) if c == 0 else None)
            stat(1)
            ffn(0)
            stat(2)
            u = AT["kva"]
            loaded(u)
            w = slot(u, KT, 288)
            for b, (c0, n) in enumerate(((0, P), (P, P), (192, QK1))):
                for k in range(KT):
                    if b == 0:
                        pe.wait_ge(S["hk_ready"], k + 1)
                    if b == 0 and k == 0:
                        pe.wait_ge(S["norm_std"], 3)
                    ins = mm(PS[0:n, b, 0:SEQ], w[:, k, c0:c0 + n], HK[:, k, :], k == 0, k == KT - 1)
            ins.then_inc(S["unit_done"], 1)
            linear(AT["dq"], [3, 4], H, SEQ, first=("h_ready", KT * 2))
            pe.wait_ge(S["kv_sq"], 5)
            for i, (b, c0) in enumerate(((0, 0), (3, SEQ))):
                for k in range(2):
                    mm(PS[:, 5, c0:c0 + SEQ], ones256, SQ[:, b + k, 0:SEQ], k == 0, k == 1)
            mm(PS[0:QK1, 6, 0:SEQ], blk[0:QK1, 0:QK1], SQ[0:QK1, 2, 0:SEQ], True, True).then_inc(S["kv_stat"], 1)
            pe.wait_ge(S["kv_norm"], 1)
            mm(PS[0:QK1, 7, 0:SEQ], rot[0:QK1, 0:QK1], KR[0:QK1, 0, :], True, True).then_inc(S["kr_rot"], 1)

            def project(s):
                c, i = s // 4, s % 4
                kv = c < 2
                u = AT["kvb"] + c if kv else AT["uq"] + c - 2
                if i == 0:
                    loaded(u)
                cols, per, rows, src = (1024, 128, NOPE, CKV) if kv else (768, QK1, QK1, QA)
                w = slot(u, 2, cols)
                if s >= 2:
                    pe.wait_ge(S["hp_scaled"], s - 1)
                for j in range(2):
                    c0 = (2 * i + j) * per
                    for k in range(2):
                        ins = mm(PS[0:rows, s % 2, j * SEQ:(j + 1) * SEQ], w[:, k, c0:c0 + rows], src[:, k, :], k == 0, k == 1)
                if kv and i == 3:
                    ins.then_inc(S["hp_proj"], 1)
                    heads = w.rearrange("p k (h c) -> p k h c", c=128)
                    if c == 0:
                        pe.wait_ge(S["kr_done"], 1)
                    else:
                        pe.wait_ge(S["v_copied"], 2)
                    for tt in range(2):
                        for k in range(2):
                            ins = mm(PS[:, 6 + tt, :], CKV[:, k, tt * P:(tt + 1) * P], heads[:, k, :, NOPE:], k == 0, k == 1)
                    ins.then_inc(S["unit_done"], 1)
                elif i == 3:
                    ins.then_inc(S["unit_done"], 1)
                else:
                    ins.then_inc(S["hp_proj"], 1)

            def mean_square(s):
                rows = NOPE if s < 8 else QK1
                pe.wait_ge(S["hp_sq"], s + 1)
                if s >= 2:
                    pe.wait_ge(S["hp_std"], s - 1)
                mm(PS[0:rows, 2 + s % 2, :], blk[0:rows, 0:rows], SQH[0:rows, s % 2, :], True, True).then_inc(S["hp_stat"], 1)

            for s in range(18):
                if s < 16:
                    project(s)
                if 1 <= s <= 16:
                    mean_square(s - 1)
                if s >= 10:
                    s1 = s - 10
                    pe.wait_ge(S["hp_scaled"], 8 + s1 + 1)
                    if s1 >= 2:
                        pe.wait_ge(S["rope_used"], s1 - 1)
                    mm(PS[0:QK1, 4 + s1 % 2, :], rot[0:QK1, 0:QK1], QH[0:QK1, 2 * s1:2 * s1 + 2, :].rearrange("p a t -> p (a t)"),
                       True, True).then_inc(S["hp_rot"], 1)
            pe.wait_ge(S["hp_done"], 8)
            pe.wait_ge(S["v_copied"], 4)
            for h in range(HEADS1 + 2):
                if h < HEADS1:
                    if h >= 2:
                        pe.wait_ge(S["s_sb"], h - 1)
                    mm(PS[:, h % 2, 0:P], QH[0:QK1, h, 0:P], KH[0:QK1, h, 0:P], True, True)
                    mm(PS[:, h % 2, P:3 * P], QH[0:QK1, h, P:], KH[0:QK1, h, :], True, True).then_inc(S["s_ready"], 1)
                if 1 <= h <= HEADS1:
                    g = h - 1
                    pe.wait_ge(S["prob_ready"], g + 1)
                    if g >= 2:
                        pe.wait_ge(S["pt_copied"], g - 1)
                    for c in range(3):
                        ins = nc.tensor.transpose(PS[:, 2 + g % 2, c * P:(c + 1) * P], SM1[:, g % 2, c * P:(c + 1) * P], ident)
                    ins.then_inc(S["pt_ready"], 1)
                if h >= 2:
                    g = h - 2
                    pe.wait_ge(S["pt_copied"], g + 1)
                    if g >= 4:
                        pe.wait_ge(S["o_copied"], g // 2 - 1)
                    r = slice(64 * (g % 2), 64 * (g % 2) + 64)
                    o = 4 + g // 2 % 2
                    mm(PS[r, o, 0:SEQ], VT[:, 0, g * VDIM:(g + 1) * VDIM], PT1[:, g % 2, 0:SEQ], True, False)
                    mm(PS[r, o, P:SEQ], VT[:, 1, g * VDIM:(g + 1) * VDIM], PT1[:, g % 2, SEQ:], False, True).then_inc(S["o_ready"], 1)
            for c in range(4):
                linear3(AT["wo"] + c, [(6 + 2 * c) % 8, (7 + 2 * c) % 8], (OAH, OAL), SEQ, first=("o_copied", 0) if c == 0 else None)
            stat(3)
            ffn(1)
            stat(4)
            ffn(2)
            stat(5)
            stat(6)
            for i, label in enumerate(("q2", "q2", "k2", "k2")):
                linear3(AT[label] + i % 2, [2 * i, 2 * i + 1], (HH, HL), TALL, first=("h_ready", KT * 5) if i == 0 else None)
            tokens = ((0, P), (P, P), (2 * P, NMETA))
            pe.wait_ge(S["qk_copied"], 2)
            for c in range(2):
                u = AT["v2"] + c
                split(u)
                w = parts(u, KT, 256)
                for tt, (t0, n) in enumerate(tokens):
                    for k in range(KT):
                        ins = mm3(PS[0:n, tt, c * 256:(c + 1) * 256], [v[:, k, t0:t0 + n] for v in (HH, HL)],
                                  [v[:, k, :] for v in w], k == 0, k == KT - 1)
                ins.then_inc(S["unit_done"], 1)
            u = AT["f2"]
            split(u)
            w = parts(u, KT, HEADS2)
            for k in range(KT):
                ins = mm3(PS[0:HEADS2, 3, 0:TALL], [v[:, k, :] for v in w], [v[:, k, :] for v in (HH, HL)], k == 0, k == KT - 1)
            ins.then_inc(S["unit_done"], 1)
            pe.wait_ge(S["qk_copied"], 4)
            for i in range(6):
                if i >= 2:
                    pe.wait_ge(S["c_copied"], i - 1)
                linear3(AT["cin"] + i, [4 + 2 * (i % 2), 5 + 2 * (i % 2)], (HH, HL), TALL)
            pe.wait_ge(S["v2_copied"], 3)
            pe.wait_ge(S["f_act"], 1)
            for i in range(8):
                if i >= 2:
                    pe.wait_ge(S["gate_ready"], i - 1)
                linear3(AT["gates"] + i, [2 * (i % 2), 1 + 2 * (i % 2)], (HH, HL), TALL)
            pe.wait_ge(S["f_ready"], 1)
            pe.wait_ge(S["gate_ready"], 8)
            for tt, (t0, n) in enumerate(tokens):
                ins = nc.tensor.transpose(PS[0:n, 3, tt * HEADS2:(tt + 1) * HEADS2], FROW[0:HEADS2, 5, t0:t0 + n],
                                          ident[0:HEADS2, 0:HEADS2])
            ins.then_inc(S["fq_ready"], 1)
            pe.wait_ge(S["u_ready"], 2)
            for h in range(HEADS2):
                if h >= 4:
                    pe.wait_ge(S["fb_copied"], h - 3)
                mm(PS[:, 4 + h % 4, 0:TALL], ident[0:HEADS2, h:h + 1].broadcast_to([HEADS2, P]), FROW[0:HEADS2, 5, :], True, True)\
                    .then_inc(S["fb_ready"], 1)
            pe.wait_ge(S["fq_copied"], 1)
            pe.wait_ge(S["fb_copied"], 8)
            for h in range(HEADS2 + 2):
                if h < HEADS2:
                    p, m = h % 2, h // 2
                    r = slice(64 * p, 64 * p + 64)
                    if h >= 2:
                        pe.wait_ge(S["s2_sb"], h - 1)
                    mm(PS[:, 2 * p, 0:P], Q2[r, m, 0:P], K2[r, m, 0:P], True, True)
                    mm(PS[:, 2 * p, P:3 * P], Q2[r, m, P:2 * P], K2[r, m, 0:2 * P], True, True)
                    mm(PS[0:NMETA, 2 * p + 1, 0:TALL], Q2[r, m, 2 * P:], K2[r, m, :], True, True).then_inc(S["s2_ready"], 1)
                if 1 <= h <= HEADS2:
                    g = h - 1
                    p = g % 2
                    pe.wait_ge(S["s2_prob"], g + 1)
                    if g >= 2:
                        pe.wait_ge(S["pt2_copied"], g - 1)
                    for kt, qt, c0 in ((0, 0, 0), (0, 1, 128), (0, 2, 256), (1, 1, 272), (1, 2, 400), (2, 2, 416)):
                        rows, keys = QT2[qt][0], (P, P, NMETA)[kt]
                        ins = nc.tensor.transpose(PS[0:keys, 4 + p, c0:c0 + rows], SM2[0:rows, p, qt, kt * P:kt * P + keys],
                                                  ident[0:rows, 0:rows])
                    ins.then_inc(S["pt2_ready"], 1)
                if h >= 2:
                    g = h - 2
                    p = g % 2
                    pe.wait_ge(S["pt2_copied"], g + 1)
                    if g >= 4:
                        pe.wait_ge(S["o2_copied"], g // 2 - 1)
                    r, o = slice(64 * p, 64 * p + 64), 6 + g // 2 % 2
                    d = slice(g * DH2, (g + 1) * DH2)
                    mm(PS[r, o, 0:TALL], V2[:, 0, d], PT2[:, p, 0:272], True, False)
                    mm(PS[r, o, P:TALL], V2[:, 1, d], PT2[:, p, 272:416], False, False)
                    mm(PS[r, o, 2 * P:TALL], V2[0:NMETA, 2, d], PT2[0:NMETA, p, 416:432], False, True).then_inc(S["o2_ready"], 1)
            for c in range(2):
                if c == 0:
                    pe.wait_ge(S["s2_sb"], HEADS2)
                linear(AT["attn_br"] + c, list(range(4 * c, 4 * c + 4)), O2, TALL, first=("o2_copied", 0) if c == 0 else None)
            pe.wait_ge(S["conv_ready"], 1)
            for c in range(2):
                pe.wait_ge(S["mix_part"], 4 * c + 4)
                linear(AT["conv_br"] + c, list(range(4 * c, 4 * c + 4)), CB, TALL)
            pe.wait_ge(S["mix_part"], 2 * KT)
            for c in range(4):
                if c >= 2:
                    pe.wait_ge(S["res_ready"], KT * R_YM + 2 * (c - 1))
                linear3(AT["w_out"] + c, [2 * (c % 2), 2 * (c % 2) + 1], (HH, HL), TALL, first=("mix_ready", 0) if c == 0 else None)
            stat(7)
            stat(8)
            ffn(3)
            stat(9)
            for b in range(4):
                for m in range(4):
                    f = 4 * (b % 2) + m
                    pe.wait_ge(S["res_ready"], KT * R_X3 + f + 1)
                    t0 = NMETA + (b // 2) * P
                    ins = nc.tensor.transpose(PS[:, b, m * P:(m + 1) * P], X[:, f, t0:t0 + P], ident)
                ins.then_inc(S["out_tr"], 1)


_INS = ["x", "c", "positions", "ada_w", "ada_b", "norm1_g", "norm2_g", "ffn_w_gate", "ffn_w_up", "ffn_w_down",
        "s5_lam_re", "s5_lam_im", "s5_log_dt", "s5_b_re", "s5_b_im", "s5_c_re", "s5_c_im", "s5_d", "s5_w_glu",
        "s5_b_glu", "kv_ada_w", "kv_ada_b", "kv_norm_g", "w_kv_a", "kv_a_norm_g", "w_kv_b", "k_nope_norm_g",
        "k_rope_norm_g", "mla_w_dq", "mla_q_norm_g", "mla_w_uq", "mla_q_nope_norm_g", "mla_q_rope_norm_g",
        "mla_w_o", "meta_tokens_2", "w_in_2", "b_forget_2", "conv_w_2", "w_attn_branch_2", "w_conv_branch_2",
        "w_out_2", "g_ffn1_pre_2", "g_ffn1_post_2", "w_ffn1_in_2", "w_ffn1_out_2", "g_mix_pre_2", "g_mix_post_2",
        "g_ffn2_pre_2", "g_ffn2_post_2", "w_ffn2_in_2", "w_ffn2_out_2"]


def kernel(**inputs):
    import concourse.bacc as _bacc
    from concourse import mybir as _mybir
    from concourse.bass_utils import run_bass_kernel_spmd as _run

    nc = _bacc.Bacc("TRN2", target_bir_lowering=False, num_devices=1)
    arrays, aps = {}, {}

    def give(name, a):
        a = np.ascontiguousarray(a)
        arrays[f"in_{name}"] = a
        aps[name] = nc.dram_tensor(f"in_{name}", a.shape, _mybir.dt.from_np(a.dtype), kind="ExternalInput").ap()

    for name in _INS:
        give(name, inputs[name])
    give("consts", constants())
    out = nc.dram_tensor("out", (1, SEQ, D), _mybir.dt.float32, kind="ExternalOutput").ap()
    build(nc, aps, out)
    return _run(nc, [arrays], core_ids=[0]).results[0]["out"]
```
